# Optimizing a Trainium2 kernel written in Bass

```python
import jax, jax.numpy as jnp
from jax import lax
import numpy as np

D_MODEL = 1024
BATCH = 1
SEQ = 256
DEPTH = 1

RET_HEADS = 4
RET_QK_DIM = 128
RET_V_DIM = 256
RET_CHUNK = 128
ROPE_BASE = 10000.0
MOBA_HEADS = 8
MOBA_HEAD_DIM = 128
MOBA_BLOCK = 256
MOBA_TOPK = 3
MOBA_Q_CHUNK = 16
D_FF = 2816
CONV_WIDTH = 3
NORM_EPS = 1e-6

RET_QK = RET_HEADS * RET_QK_DIM
RET_V = RET_HEADS * RET_V_DIM
MOBA_W = MOBA_HEADS * MOBA_HEAD_DIM
IN_SPLITS = (RET_QK, RET_QK, RET_V, RET_V, MOBA_W, MOBA_W, MOBA_W)
D_IN = RET_QK * 2 + RET_V * 2 + MOBA_W * 3

kernel_name = "hybrid_retention_moba_convffn"

def rms_norm(x, gain):
    xf = x.astype(jnp.float32)
    inv = lax.rsqrt(jnp.mean(xf * xf, axis=-1, keepdims=True) + NORM_EPS)
    return (xf * inv).astype(x.dtype) * gain

def rotary(x, pos):
    d = x.shape[-1]
    half = d // 2
    inv_freq = ROPE_BASE ** (-jnp.arange(half, dtype=jnp.float32) / half)
    ang = pos.astype(jnp.float32)[:, None] * inv_freq[None, :]
    cos = jnp.cos(ang).astype(x.dtype)
    sin = jnp.sin(ang).astype(x.dtype)
    x1, x2 = x[..., :half], x[..., half:]
    return jnp.concatenate([x1 * cos - x2 * sin, x1 * sin + x2 * cos], axis=-1)

def retention_chunkwise(q, k, v):
    B, H, S, dk = q.shape
    dv = v.shape[-1]
    C = RET_CHUNK
    n = S // C
    dt = q.dtype
    log_gamma = jnp.log1p(-jnp.power(2.0, -5.0 - jnp.arange(H, dtype=jnp.float32)))
    pos = jnp.arange(C, dtype=jnp.float32)
    diff = pos[:, None] - pos[None, :]
    decay_in = jnp.where(diff >= 0, jnp.exp(log_gamma[:, None, None] * jnp.maximum(diff, 0.0)), 0.0).astype(dt)
    zeta = jnp.exp(log_gamma[:, None] * (C - 1 - pos)[None, :]).astype(dt)
    xi = jnp.exp(log_gamma[:, None] * (pos + 1)[None, :]).astype(dt)
    gamma_c = jnp.exp(log_gamma * C).astype(dt)
    qc = q.reshape(B, H, n, C, dk)
    kc = k.reshape(B, H, n, C, dk)
    vc = v.reshape(B, H, n, C, dv)
    scores = jnp.einsum('bhncd,bhnmd->bhncm', qc, kc) * decay_in[None, :, None]
    o_inner = jnp.einsum('bhncm,bhnme->bhnce', scores, vc)
    kv = jnp.einsum('bhnmd,hm,bhnme->bhnde', kc, zeta, vc)

    def step(R, kv_n):
        return gamma_c[None, :, None, None] * R + kv_n, R

    _, r_prev = lax.scan(step, jnp.zeros((B, H, dk, dv), dt), jnp.moveaxis(kv, 2, 0))
    r_prev = jnp.moveaxis(r_prev, 0, 2)
    o_cross = jnp.einsum('bhncd,hc,bhnde->bhnce', qc, xi, r_prev)
    return (o_inner + o_cross).reshape(B, H, S, dv)

def head_group_norm(o, gain, bias):
    B, H, S, dv = o.shape
    of = o.astype(jnp.float32)
    mu = jnp.mean(of, axis=-1, keepdims=True)
    var = jnp.mean(jnp.square(of - mu), axis=-1, keepdims=True)
    on = ((of - mu) * lax.rsqrt(var + NORM_EPS)).astype(o.dtype)
    on = on.transpose(0, 2, 1, 3).reshape(B, S, H * dv)
    return on * gain + bias

def moba_attention(q, k, v):
    B, H, S, d = q.shape
    nb = -(-S // MOBA_BLOCK)
    s_pad = nb * MOBA_BLOCK
    padw = ((0, 0), (0, 0), (0, s_pad - S), (0, 0))
    q, k, v = jnp.pad(q, padw), jnp.pad(k, padw), jnp.pad(v, padw)
    kb = k.reshape(B, H, nb, MOBA_BLOCK, d)
    vb = v.reshape(B, H, nb, MOBA_BLOCK, d)
    k_mean = jnp.mean(kb.astype(jnp.float32), axis=3).astype(k.dtype)
    top = min(MOBA_TOPK, nb)
    scale = MOBA_HEAD_DIM ** -0.5
    n_chunks = s_pad // MOBA_Q_CHUNK
    q_chunks = jnp.moveaxis(q.reshape(B, H, n_chunks, MOBA_Q_CHUNK, d), 2, 0)
    b_ix = jnp.arange(B)[:, None, None, None]
    h_ix = jnp.arange(H)[None, :, None, None]
    blk_ids = jnp.arange(nb)
    slot_ids = jnp.arange(top)

    def one_chunk(args):
        i, q_i = args
        start = i * MOBA_Q_CHUNK
        own = start // MOBA_BLOCK
        t = start + jnp.arange(MOBA_Q_CHUNK)
        gate = jnp.einsum('bhqd,bhnd->bhqn', q_i, k_mean).astype(jnp.float32)
        gate = jnp.where(blk_ids < own, gate, -jnp.inf)
        _, gidx = lax.top_k(gate, top)
        valid = slot_ids < own
        gidx = jnp.where(valid, gidx, 0)
        k_sel = kb[b_ix, h_ix, gidx]
        v_sel = vb[b_ix, h_ix, gidx]
        s_sel = jnp.einsum('bhqd,bhqnkd->bhqnk', q_i, k_sel).astype(jnp.float32) * scale
        s_sel = jnp.where(valid[:, None], s_sel, -jnp.inf).reshape(B, H, MOBA_Q_CHUNK, top * MOBA_BLOCK)
        k_own = lax.dynamic_slice_in_dim(k, own * MOBA_BLOCK, MOBA_BLOCK, axis=2)
        v_own = lax.dynamic_slice_in_dim(v, own * MOBA_BLOCK, MOBA_BLOCK, axis=2)
        kpos = own * MOBA_BLOCK + jnp.arange(MOBA_BLOCK)
        s_own = jnp.einsum('bhqd,bhkd->bhqk', q_i, k_own).astype(jnp.float32) * scale
        s_own = jnp.where(kpos[None, :] <= t[:, None], s_own, -jnp.inf)
        p = jax.nn.softmax(jnp.concatenate([s_sel, s_own], axis=-1), axis=-1).astype(v.dtype)
        p_sel = p[..., :top * MOBA_BLOCK].reshape(B, H, MOBA_Q_CHUNK, top, MOBA_BLOCK)
        p_own = p[..., top * MOBA_BLOCK:]
        return (jnp.einsum('bhqnk,bhqnkd->bhqd', p_sel, v_sel)
                + jnp.einsum('bhqk,bhkd->bhqd', p_own, v_own))

    out = lax.map(one_chunk, (jnp.arange(n_chunks), q_chunks))
    out = jnp.moveaxis(out, 0, 2).reshape(B, H, s_pad, d)
    return out[:, :, :S]

def causal_depthwise_conv(h, w, b):
    S = h.shape[1]
    hp = jnp.pad(h, ((0, 0), (CONV_WIDTH - 1, 0), (0, 0)))
    out = b + w[0] * hp[:, 0:S]
    for i in range(1, CONV_WIDTH):
        out = out + w[i] * hp[:, i:i + S]
    return out

def setup_inputs(seed: int = 0) -> dict:
    key = jax.random.key(seed)
    ks = jax.random.split(key, 18)
    f32 = jnp.float32

    def nrm(k, shape, fan_in):
        return jax.random.normal(k, shape, f32) * (fan_in ** -0.5)

    def gain(k, shape):
        return 1.0 + 0.02 * jax.random.normal(k, shape, f32)

    def small(k, shape):
        return 0.02 * jax.random.normal(k, shape, f32)

    L = DEPTH
    return {
        "x": jax.random.normal(ks[0], (BATCH, SEQ, D_MODEL), f32),
        "attn_norm": gain(ks[1], (L, D_MODEL)),
        "w_in": nrm(ks[2], (L, D_MODEL, D_IN), D_MODEL),
        "ret_norm_gain": gain(ks[3], (L, RET_V)),
        "ret_norm_bias": small(ks[4], (L, RET_V)),
        "moba_q_gain": gain(ks[5], (L, MOBA_HEAD_DIM)),
        "moba_k_gain": gain(ks[6], (L, MOBA_HEAD_DIM)),
        "w_ret_o": nrm(ks[7], (L, RET_V, D_MODEL), RET_V),
        "w_moba_o": nrm(ks[8], (L, MOBA_W, D_MODEL), MOBA_W),
        "w_gate": nrm(ks[9], (L, D_MODEL, 2 * D_MODEL), D_MODEL),
        "b_gate": small(ks[10], (L, 2 * D_MODEL)),
        "w_out": nrm(ks[11], (L, D_MODEL, D_MODEL), D_MODEL),
        "ffn_norm": gain(ks[12], (L, D_MODEL)),
        "w_up": nrm(ks[13], (L, D_MODEL, 2 * D_FF), D_MODEL),
        "conv_w": nrm(ks[14], (L, CONV_WIDTH, 2 * D_FF), CONV_WIDTH),
        "conv_b": small(ks[15], (L, 2 * D_FF)),
        "w_down": nrm(ks[16], (L, D_FF, D_MODEL), D_FF),
    }

def reference(x, attn_norm, w_in, ret_norm_gain, ret_norm_bias, moba_q_gain, moba_k_gain,
              w_ret_o, w_moba_o, w_gate, b_gate, w_out, ffn_norm, w_up, conv_w, conv_b, w_down):
    B, S, _ = x.shape
    pos = jnp.arange(S)
    offsets = tuple(int(o) for o in np.cumsum(IN_SPLITS)[:-1])

    def heads(t, nh):
        return t.reshape(B, S, nh, -1).transpose(0, 2, 1, 3)

    for l in range(DEPTH):
        h = rms_norm(x, attn_norm[l])
        proj = h @ w_in[l]
        q_r, k_r, v_r, g_r, q_m, k_m, v_m = jnp.split(proj, offsets, axis=-1)
        qr = rotary(heads(q_r, RET_HEADS), pos)
        kr = rotary(heads(k_r, RET_HEADS), pos) * (RET_QK_DIM ** -0.5)
        o_r = retention_chunkwise(qr, kr, heads(v_r, RET_HEADS))
        o_r = head_group_norm(o_r, ret_norm_gain[l], ret_norm_bias[l]) * jax.nn.silu(g_r)
        y_ret = o_r @ w_ret_o[l]
        qm = rms_norm(heads(q_m, MOBA_HEADS), moba_q_gain[l])
        km = rms_norm(heads(k_m, MOBA_HEADS), moba_k_gain[l])
        o_m = moba_attention(qm, km, heads(v_m, MOBA_HEADS))
        y_moba = o_m.transpose(0, 2, 1, 3).reshape(B, S, MOBA_W) @ w_moba_o[l]
        gates = jax.nn.sigmoid(h @ w_gate[l] + b_gate[l])
        gate_ret, gate_moba = jnp.split(gates, 2, axis=-1)
        x = x + (gate_ret * y_ret + gate_moba * y_moba) @ w_out[l]
        h = rms_norm(x, ffn_norm[l])
        u = causal_depthwise_conv(h @ w_up[l], conv_w[l], conv_b[l])
        u_gate, u_val = jnp.split(u, 2, axis=-1)
        x = x + (jax.nn.silu(u_gate) * u_val) @ w_down[l]
    return x


_drawn_inputs = setup_inputs


def setup_inputs(seed=0):
    import zlib

    import numpy as np

    out = dict(_drawn_inputs(seed))
    spreads = {}
    factors = {'attn_norm': 3.532,
     'ret_norm_gain': 8.0,
     'ret_norm_bias': 8.0,
     'moba_q_gain': 8.0,
     'moba_k_gain': 8.0,
     'b_gate': 8.0,
     'ffn_norm': 12.365,
     'conv_b': 12.013}
    for name, (base, spread) in spreads.items():
        noise = np.random.default_rng([zlib.crc32(name.encode()), seed]).standard_normal(out[name].shape)
        drawn = base * np.exp(spread * noise) if base else spread * noise
        out[name] = __import__('jax').numpy.asarray(drawn.astype(out[name].dtype))
    for name, factor in factors.items():
        out[name] = (out[name] * factor).astype(out[name].dtype)
    return out
```

```python
import math

import numpy as np

import concourse.bass as bass
from concourse import mybir
from contextlib import ExitStack

P = 128
SEQ, D = 256, 1024
NT = SEQ // P
KT = D // P
RET_HEADS, RET_QK, RET_V = 4, 128, 256
MOBA_HEADS, HEAD = 8, 128
D_FF = 2816
EPS = 1e-6
BLOCK_COLS = 512
HALF_ELEMS = 2048
SLOTS = 4
UP_COLS = 256
UP_BLOCKS = D_FF // UP_COLS
DOWN_HALVES = D_FF // P // 2
QK_SCALE = 1.0 / math.sqrt(HEAD)
MASKED = -3.0e38

(Q_R, K_R, V_R0, V_R1, G_R0, G_R1, Q_M0, Q_M1, K_M0, K_M1, V_M0, V_M1,
 GATE_R0, GATE_R1, RET_O0, RET_O1, GATE_M0, GATE_M1, MOBA_O0, MOBA_O1,
 OUT0, OUT1, UP0) = range(23)
DOWN_FIRST_HALF = 2 * (UP0 + UP_BLOCKS)
HALVES = DOWN_FIRST_HALF + DOWN_HALVES

UNITS = {}
for _name, _count in (("h", 4), ("q_r", 2), ("k_r", 2), ("ret_scores", 4), ("ret_out", 4), ("q_m0", 2),
                      ("q_m1", 2), ("ret_t", 4), ("k_m0", 2), ("k_m1", 2), ("scores0", 4), ("scores1", 4),
                      ("probs0", 4), ("moba_out0", 2), ("probs1", 4), ("moba_out1", 2), ("h2", 4)):
    UNITS[_name] = (sum(c for _, c in UNITS.values()), _count)


def unit(name, j):
    return UNITS[name][0] + j


COL_Q_GAIN, COL_K_GAIN, COL_RET_GAIN, COL_RET_BIAS, COL_GATE_BIAS, COL_CONV = 0, 1, 2, 10, 18, 34
CONV_COLS = 16 * UP_BLOCKS
COLS = COL_CONV + CONV_COLS


def hybrid_layer(nc, x, weights, gain_rows, cols, ident_in, mask_in, rotary_in, decay_in, out):
    f32 = mybir.dt.float32
    f32r = mybir.dt.float32r
    ALU = mybir.AluOpType
    ACT = mybir.ActivationFunctionType

    x_view = x.rearrange("(t p) d -> p t d", p=P)
    out_view = out.rearrange("(t p) d -> p t d", p=P)

    with ExitStack() as ctx:
        def sb(name, shape, dt=f32):
            return ctx.enter_context(nc.sbuf_tensor(name, shape, dt))

        def sem(name):
            return ctx.enter_context(nc.semaphore(name))

        raw = [sb(f"w_raw{r}", [P, HALF_ELEMS]) for r in range(SLOTS)]
        w_hi = [sb(f"w_hi{r}", [P, HALF_ELEMS], f32r) for r in range(SLOTS)]
        w_lo = [sb(f"w_lo{r}", [P, HALF_ELEMS], f32r) for r in range(SLOTS)]
        h_hi = sb("h_hi", [P, KT, SEQ], f32r)
        h_lo = sb("h_lo", [P, KT, SEQ], f32r)
        a_hi = sb("a_hi", [P, D_FF // P, SEQ], f32r)
        a_lo = sb("a_lo", [P, D_FF // P, SEQ], f32r)
        area = sb("area", [P, 8192])
        xs = sb("xs", [P, 2048])
        ys = sb("ys", [P, 2048])
        ident = sb("ident", [P, P])
        mask = sb("mask", [P, 2 * P])
        col = sb("col", [P, COLS])
        ss_x = sb("ss_x", [P, 2])
        inv_x = sb("inv_x", [P, 2])
        ss_qk = sb("ss_qk", [P, 4, 8])
        inv_qk = sb("inv_qk", [P, 4, 8])
        gn_stats = sb("gn_stats", [P, 8, 6])
        gn_mv = sb("gn_mv", [P, 8, 2])
        gn_rstd = sb("gn_rstd", [P, 8])
        neg_half = sb("neg_half", [P, 8])
        row_max = sb("row_max", [P, 16])
        neg_max = sb("neg_max", [P, 16])
        row_sum = sb("row_sum", [P, 16])
        inv_sum = sb("inv_sum", [P, 16])
        ss_x2 = sb("ss_x2", [P, 4])
        inv_x2 = sb("inv_x2", [P, 2])

        cos_t = area[:, 0:256].rearrange("p (t d) -> p t d", t=NT)
        sin_t = area[:, 256:512].rearrange("p (t d) -> p t d", t=NT)
        rotary = area[:, 0:512]
        decay = area[:, 512:2048]
        ret_t = area[:, 0:2048].rearrange("p (k s) -> p k s", k=KT)
        gates = area[:, 0:2048].rearrange("p (k s) -> p k s", k=KT)
        qr_t = area[:, 2048:3072].rearrange("p (h s) -> p h s", h=RET_HEADS)
        kr_t = area[:, 3072:4096].rearrange("p (h s) -> p h s", h=RET_HEADS)
        v_r = area[:, 4096:6144].rearrange("p (t d) -> p t d", t=NT)
        qm_t = area[:, 2048:4096].rearrange("p (h s) -> p h s", h=MOBA_HEADS)
        km_t = area[:, 4096:6144].rearrange("p (h s) -> p h s", h=MOBA_HEADS)
        g_t = area[:, 6144:8192].rearrange("p (k s) -> p k s", k=KT)
        v_m = area[:, 6144:8192].rearrange("p (t d) -> p t d", t=NT)
        probs_t = area[:, 2048:5120].rearrange("p (h s) -> p h s", h=MOBA_HEADS)
        gain_row = area[:, 5120:6144]
        PAD = 2
        u_in = area[:, 0:2 * 4 * (PAD + SEQ)].rearrange("p (b m s) -> p b m s", b=2, m=4)
        conv = area[:, 2064:2064 + 2048].rearrange("p (b m s) -> p b m s", b=2, m=4)
        discard = a_hi[:, 2 * KT:2 * KT + 4, :].rearrange("p k (i c) -> p (k i) c", c=P)
        prod = area[:, 6144:7168].rearrange("p (b m s) -> p b m s", b=2, m=2)
        x_tok = xs[:, :].rearrange("p (t d) -> p t d", t=NT)
        y_tok = ys[:, :].rearrange("p (t d) -> p t d", t=NT)
        rot = ys[:, :].rearrange("p (b t d) -> p b t d", b=2, t=NT)
        qn = xs[:, :].rearrange("p (b t d) -> p b t d", b=2, t=NT)
        ret_probs = xs[:, 0:1536].rearrange("p (h s) -> p h s", h=4)
        probs = [xs[:, 0:1536].rearrange("p (h s) -> p h s", h=4),
                 ys[:, 0:1536].rearrange("p (h s) -> p h s", h=4)]
        merged = ys[:, :].rearrange("p (k s) -> p k s", k=KT)

        bank = [ctx.enter_context(nc.psum_tensor(f"bank{i}", [P, 512], f32)) for i in range(8)]

        raw_loaded = [sem(f"raw_loaded{r}") for r in range(SLOTS)]
        hi_ready = sem("hi_ready")
        lo_ready = sem("lo_ready")
        half_used = sem("half_used")
        bank_read = [sem(f"bank_read{s}") for s in range(2)]
        unit_made = sem("unit_made")
        unit_read = [sem(f"unit_read{k}") for k in range(4)]
        x_loaded = [sem(f"x_loaded{t}") for t in range(NT)]
        gain_loaded = sem("gain_loaded")
        ident_loaded = sem("ident_loaded")
        rotary_loaded = sem("rotary_loaded")
        tables_loaded = sem("tables_loaded")
        x_again = sem("x_again")
        gain2_loaded = sem("gain2_loaded")
        sums_x = sem("sums_x")
        inv_x_ready = sem("inv_x_ready")
        xn_ready = sem("xn_ready")
        h_hi_ready = sem("h_hi_ready")
        rot_ready = sem("rot_ready")
        gn_stats_ready = sem("gn_stats_ready")
        gn_rstd_ready = sem("gn_rstd_ready")
        sums_qk = sem("sums_qk")
        inv_qk_ready = sem("inv_qk_ready")
        ret_affine = sem("ret_affine")
        ret_gated = sem("ret_gated")
        ret_hi_ready = sem("ret_hi_ready")
        ret_split = sem("ret_split")
        neg_max_ready = sem("neg_max_ready")
        exp_done = sem("exp_done")
        probs_ready = sem("probs_ready")
        attn_hi_ready = sem("attn_hi_ready")
        merged_ready = sem("merged_ready")
        merged_hi_ready = sem("merged_hi_ready")
        merged_split = sem("merged_split")
        out_chunk0 = sem("out_chunk0")
        sums_x2 = sem("sums_x2")
        inv_x2_ready = sem("inv_x2_ready")
        xn2_ready = sem("xn2_ready")
        h2_hi_ready = sem("h2_hi_ready")
        pads_zero = sem("pads_zero")
        conv_gate_done = sem("conv_gate_done")
        silu_done = sem("silu_done")
        prod_ready = sem("prod_ready")
        a_hi_ready = sem("a_hi_ready")
        a_split = sem("a_split")
        down_chunk0 = sem("down_chunk0")
        out_ready = sem("out_ready")
        stored = sem("stored")
        dve_step = sem("dve_step")
        pool_step = sem("pool_step")

        def ubank(u):
            return bank[4 + u % 4]

        def wait_unit_read(eng, u):
            eng.wait_ge(unit_read[u % 4], u // 4 + 1)

        def wait_bank_read(eng, b, j):
            eng.wait_ge(bank_read[b % 2], 2 * (b // 2) + j + 1)

        def block_bank(b, j):
            return bank[2 * (b % 2) + j]

        block = ctx.enter_context(nc.Block())

        @block.sync
        def _(sp):
            for t in range(NT):
                sp.dma_start(x_tok[:, t, :], x_view[:, t, :]).then_inc(x_loaded[t], 16)
            for r in range(SLOTS):
                sp.dma_start(raw[r][:, :], weights[r]).then_inc(raw_loaded[r], 16)
            ROUNDS = (HALVES - SLOTS) // SLOTS
            with sp.Fori(0, ROUNDS) as i:
                for r in range(SLOTS):
                    sp.wait_ge(lo_ready, i * SLOTS + (r + 1))
                    sp.dma_start(raw[r][:, :], weights[i * SLOTS + (r + SLOTS)]).then_inc(raw_loaded[r], 16)
            for n in range(SLOTS * (ROUNDS + 1), HALVES):
                sp.wait_ge(lo_ready, n - SLOTS + 1)
                sp.dma_start(raw[n % SLOTS][:, :], weights[n]).then_inc(raw_loaded[n % SLOTS], 16)
            for t in range(NT):
                for n in range(2):
                    sp.wait_ge(out_ready, 2 * t + n + 1)
                    sp.dma_start(out_view[:, t, 512 * n:512 * n + 512],
                                 y_tok[:, t, 512 * n:512 * n + 512]).then_inc(stored, 16)
            sp.wait_ge(stored, 16 * 4)

        @block.gpsimd
        def _(pool):
            done = [0]

            def step(ins):
                done[0] += 1
                ins.then_inc(pool_step, 1)
                pool.wait_ge(pool_step, done[0])

            def inv_sqrt(dst, src, factor, width):
                step(nc.gpsimd.tensor_scalar(dst, src, factor, EPS, ALU.mult, ALU.add))
                return nc.gpsimd.tensor_tensor(dst, dst, neg_half[:, 0:width], ALU.pow)

            step(nc.gpsimd.memset(neg_half[:, :], -0.5))
            for t in range(NT):
                pool.wait_ge(sums_x, t + 1)
                inv_sqrt(inv_x[:, t:t + 1], ss_x[:, t:t + 1], 1.0 / D, 1).then_inc(inv_x_ready, 1)
            pool.wait_ge(gn_stats_ready, 1)
            inv_sqrt(gn_rstd[:, :], gn_mv[:, :, 1], 1.0, 8).then_inc(gn_rstd_ready, 1)
            for q in range(4):
                pool.wait_ge(sums_qk, 2 * (q + 1))
                inv_sqrt(inv_qk[:, q, :], ss_qk[:, q, :], 1.0 / HEAD, 8).then_inc(inv_qk_ready, 1)
            pool.wait_ge(unit_made, unit("probs0", 3) + 1)
            pool.dma_start(x_tok, x_view).then_inc(x_again, 16)
            pool.dma_start(gain_row, gain_rows[1:2, :].partition_broadcast(P)).then_inc(gain2_loaded, 16)
            for t in range(NT):
                pool.wait_ge(sums_x2, 3 + t)
                step(nc.gpsimd.tensor_tensor(inv_x2[:, t:t + 1], ss_x2[:, t:t + 1], ss_x2[:, 2 + t:3 + t], ALU.add))
                inv_sqrt(inv_x2[:, t:t + 1], inv_x2[:, t:t + 1], 1.0 / D, 1).then_inc(inv_x2_ready, 1)

        @block.tensor
        def _(pe):
            mm = nc.tensor.matmul

            def wait_bank_free(b):
                if b >= 2:
                    wait_bank_read(pe, b - 2, 1)

            def start_unit(name, j):
                u = unit(name, j)
                if u >= 4:
                    wait_unit_read(pe, u - 4)
                return ubank(u)

            def token_half(out_banks, n, tiles, first, last, order=None, chunk0=None):
                hi = w_hi[n % SLOTS][:, :].rearrange("p (k c) -> p k c", k=4)
                lo = w_lo[n % SLOTS][:, :].rearrange("p (k c) -> p k c", k=4)
                pairs = order or [(kk, t) for kk in range(4) for t in range(NT)]
                for kk, t in pairs:
                    k = tiles[kk]
                    s_hi = h_hi[:, k, P * t:P * t + P]
                    s_lo = h_lo[:, k, P * t:P * t + P]
                    o = out_banks[t][:, :]
                    mm(o, s_hi, hi[:, kk, :], start=(first and kk == 0), stop=False)
                    mm(o, s_hi, lo[:, kk, :], start=False, stop=False)
                    ins = mm(o, s_lo, hi[:, kk, :], start=False, stop=(last and kk == 3))
                    if chunk0 is not None and (kk, t) == (3, 0):
                        ins.then_inc(chunk0, 1)
                return ins

            def token_block(b):
                for h in range(2):
                    n = 2 * b + h
                    pe.wait_ge(lo_ready, n + 1)
                    if b == 0:
                        wait_unit_read(pe, unit("h", 2 + h))
                    if h == 0:
                        wait_bank_free(b)
                    token_half([block_bank(b, t) for t in range(NT)], n, range(4 * h, 4 * h + 4), h == 0, h == 1)\
                        .then_inc(half_used, 1)

            def channel_half(banks, slot, r_hi, r_lo, h):
                hi = w_hi[slot][:, :].rearrange("p (k c) -> p k c", k=4)
                lo = w_lo[slot][:, :].rearrange("p (k c) -> p k c", k=4)
                for m in range(4):
                    o = banks[m // 2][:, SEQ * (m % 2):SEQ * (m % 2) + SEQ]
                    for kk in range(4):
                        k = 4 * h + kk
                        s_hi, s_lo = hi[:, kk, P * m:P * m + P], lo[:, kk, P * m:P * m + P]
                        mm(o, s_hi, r_hi[:, k, :], start=(k == 0 and m % 2 == 0), stop=False)
                        mm(o, s_hi, r_lo[:, k, :], start=False, stop=False)
                        ins = mm(o, s_lo, r_hi[:, k, :], start=False, stop=(k == KT - 1 and m % 2 == 1))
                return ins

            def channel_block(b, r_hi, r_lo):
                for h in range(2):
                    n = 2 * b + h
                    pe.wait_ge(lo_ready, n + 1)
                    if h == 0:
                        wait_bank_free(b)
                    channel_half([block_bank(b, 0), block_bank(b, 1)], n % SLOTS, r_hi, r_lo, h)\
                        .then_inc(half_used, 1)

            def transposes(name, j, pieces):
                o = start_unit(name, j)
                for c, piece in enumerate(pieces):
                    ins = nc.tensor.transpose(o[:, P * c:P * c + P], piece, ident[:, :])
                ins.then_inc(unit_made, 1)

            def head_transposes(name, b, src):
                for t in range(NT):
                    wait_bank_read(pe, b, t) if name[2] == "m" else pe.wait_ge(rot_ready, 2 * b + t + 1)
                    transposes(name, t, [src[:, t, P * h:P * h + P] for h in range(4)])

            pe.wait_ge(ident_loaded, 16)
            for t in range(NT):
                for kh in range(2):
                    pe.wait_ge(xn_ready, 2 * t + kh + 1)
                    transposes("h", 2 * t + kh, [y_tok[:, t, P * k:P * k + P] for k in range(4 * kh, 4 * kh + 4)])

            def tail_ret_scores():
                for h in range(RET_HEADS):
                    if h == 0:
                        wait_unit_read(pe, unit("q_r", 1))
                        wait_unit_read(pe, unit("k_r", 1))
                    o = start_unit("ret_scores", h)
                    mm(o[:, 0:SEQ], kr_t[:, h, 0:P], qr_t[:, h, :], start=True, stop=False)
                    mm(o[:, SEQ:SEQ + P], kr_t[:, h, P:SEQ], qr_t[:, h, P:SEQ], start=False, stop=True)\
                        .then_inc(unit_made, 1)

            def tail_ret_out():
                wait_bank_read(pe, V_R0, 1)
                wait_bank_read(pe, V_R1, 1)
                for h in range(RET_HEADS):
                    wait_unit_read(pe, unit("ret_scores", h))
                    o = start_unit("ret_out", h)
                    v0, v1 = (v_r[:, t, RET_V * h:RET_V * h + RET_V] for t in range(NT))
                    mm(o[:, 0:RET_V], ret_probs[:, h, 0:P], v0, start=True, stop=False)
                    mm(o[:, RET_V:2 * RET_V], ret_probs[:, h, P:SEQ], v0, start=False, stop=False)
                    mm(o[:, RET_V:2 * RET_V], ret_probs[:, h, SEQ:SEQ + P], v1, start=False, stop=True)\
                        .then_inc(unit_made, 1)

            def tail_ret_transpose():
                for h in range(RET_HEADS):
                    wait_unit_read(pe, unit("ret_out", h))
                for j in range(4):
                    transposes("ret_t", j, [y_tok[:, t, P * k:P * k + P] for k in (2 * j, 2 * j + 1) for t in range(NT)])

            def tail_scores(g):
                for j in range(4):
                    h = 4 * g + j
                    if j == 0:
                        for which in ("q_m", "k_m"):
                            wait_unit_read(pe, unit(f"{which}{g}", 1))
                    o = start_unit(f"scores{g}", j)
                    mm(o[:, 0:P], qm_t[:, h, 0:P], km_t[:, h, 0:P], start=True, stop=False)
                    mm(o[:, P:P + SEQ], qm_t[:, h, P:SEQ], km_t[:, h, :], start=False, stop=True)\
                        .then_inc(unit_made, 1)

            def tail_probs(g):
                for j in range(4):
                    pe.wait_ge(probs_ready, 4 * g + j + 1)
                    transposes(f"probs{g}", j, [probs[g][:, j, P * c:P * c + P] for c in range(3)])

            def tail_moba_out(g):
                if g == 0:
                    wait_bank_read(pe, V_M0, 1)
                    wait_bank_read(pe, V_M1, 1)
                for j in range(2):
                    o = start_unit(f"moba_out{g}", j)
                    for i in range(2):
                        h = 4 * g + 2 * j + i
                        wait_unit_read(pe, unit(f"probs{g}", 2 * j + i))
                        v0, v1 = (v_m[:, t, HEAD * h:HEAD * h + HEAD] for t in range(NT))
                        mm(o[:, SEQ * i:SEQ * i + SEQ], v0, probs_t[:, h, 0:SEQ], start=(i == 0), stop=False)
                        ins = mm(o[:, SEQ * i + P:SEQ * i + SEQ], v1, probs_t[:, h, SEQ:SEQ + P],
                                 start=False, stop=(i == 1))
                    ins.then_inc(unit_made, 1)

            token_block(Q_R)
            token_block(K_R)
            head_transposes("q_r", 0, rot[:, 0])
            token_block(V_R0)
            head_transposes("k_r", 1, rot[:, 1])
            token_block(V_R1)
            tail_ret_scores()
            channel_block(G_R0, h_hi, h_lo)
            tail_ret_out()
            channel_block(G_R1, h_hi, h_lo)
            token_block(Q_M0)
            token_block(Q_M1)
            head_transposes("q_m0", Q_M0, qn[:, 0])
            token_block(K_M0)
            head_transposes("q_m1", Q_M1, qn[:, 1])
            tail_ret_transpose()
            token_block(K_M1)
            head_transposes("k_m0", K_M0, qn[:, 0])
            token_block(V_M0)
            head_transposes("k_m1", K_M1, qn[:, 1])
            token_block(V_M1)
            tail_scores(0)
            channel_block(GATE_R0, h_hi, h_lo)
            tail_scores(1)
            channel_block(GATE_R1, h_hi, h_lo)
            tail_probs(0)
            pe.wait_ge(ret_split, 4)
            channel_block(RET_O0, a_hi, a_lo)
            tail_moba_out(0)
            tail_probs(1)
            channel_block(RET_O1, a_hi, a_lo)
            tail_moba_out(1)
            channel_block(GATE_M0, h_hi, h_lo)
            channel_block(GATE_M1, h_hi, h_lo)
            wait_unit_read(pe, unit("moba_out1", 1))
            channel_block(MOBA_O0, a_hi[:, KT:2 * KT], a_lo[:, KT:2 * KT])
            channel_block(MOBA_O1, a_hi[:, KT:2 * KT], a_lo[:, KT:2 * KT])

            for n in range(2 * OUT0, 2 * OUT0 + 4):
                q = n - 2 * OUT0
                pe.wait_ge(lo_ready, n + 1)
                pe.wait_ge(merged_split, 2 if q < 2 else 4)
                if q < 2:
                    wait_bank_free(OUT0 + q)
                tiles = range(4) if q < 2 else range(4, 8)
                order = [(kk, t) for t in range(NT) for kk in range(4)] if q == 3 else None
                token_half([block_bank(OUT0 + q % 2, t) for t in range(NT)], n, tiles, q < 2, q >= 2, order,
                           out_chunk0 if q == 3 else None).then_inc(half_used, 1)
            for t in range(NT):
                for kh in range(2):
                    pe.wait_ge(xn2_ready, 2 * t + kh + 1)
                    transposes("h2", 2 * t + kh, [y_tok[:, t, P * k:P * k + P] for k in range(4 * kh, 4 * kh + 4)])

            def up_half(b, n, free, slot, jj, h):
                pe.wait_ge(lo_ready, n + 1)
                if h == 0:
                    pe.wait_ge(bank_read[jj], free)
                channel_half([bank[2 * jj], bank[2 * jj + 1]], slot, h_hi, h_lo, h).then_inc(half_used, 1)

            for kh in range(2):
                wait_unit_read(pe, unit("h2", 2 + kh))
            with pe.Fori(0, UP_BLOCKS // 2) as i:
                for jj in range(2):
                    for h in range(2):
                        up_half(UP0, i * 4 + (2 * UP0 + 2 * jj + h), i * 2 + UP0, 2 * jj + h, jj, h)
            for h in range(2):
                up_half(UP0 + UP_BLOCKS - 1, DOWN_FIRST_HALF - 2 + h, UP0 + UP_BLOCKS - 1, h, 0, h)

            for j in range(DOWN_HALVES):
                n = DOWN_FIRST_HALF + j
                pe.wait_ge(lo_ready, n + 1)
                pe.wait_ge(a_split, j + 1)
                hi = w_hi[n % SLOTS][:, :].rearrange("p (k n c) -> p k n c", k=2, n=2)
                lo = w_lo[n % SLOTS][:, :].rearrange("p (k n c) -> p k n c", k=2, n=2)
                last = j == DOWN_HALVES - 1
                pairs = [(kk, t) for t in range(NT) for kk in range(2)] if last else \
                        [(kk, t) for kk in range(2) for t in range(NT)]
                for kk, t in pairs:
                    k = 2 * j + kk
                    s_hi, s_lo = (a[:, k, P * t:P * t + P] for a in (a_hi, a_lo))
                    for c in range(2):
                        mm(bank[4 + 2 * t + c][:, :], s_hi, hi[:, kk, c, :], start=(k == 0), stop=False)
                        mm(bank[4 + 2 * t + c][:, :], s_hi, lo[:, kk, c, :], start=False, stop=False)
                    for c in range(2):
                        ins = mm(bank[4 + 2 * t + c][:, :], s_lo, hi[:, kk, c, :], start=False,
                                 stop=(k == D_FF // P - 1))
                    if last and (kk, t) == (1, 0):
                        ins.then_inc(down_chunk0, 1)
                ins.then_inc(half_used, 1)

        @block.scalar
        def _(act):
            A = nc.scalar.activation

            act.dma_start(ident[:, :], ident_in).then_inc(ident_loaded, 16)
            act.dma_start(gain_row, gain_rows[0:1, :].partition_broadcast(P)).then_inc(gain_loaded, 16)
            act.dma_start(rotary, rotary_in).then_inc(rotary_loaded, 16)
            act.dma_start(decay, decay_in).then_inc(tables_loaded, 16)
            act.dma_start(mask[:, :], mask_in).then_inc(tables_loaded, 16)
            act.dma_start(col[:, :], cols).then_inc(tables_loaded, 16)

            def split(n, r=None, count=None):
                r = n % SLOTS if r is None else r
                act.wait_ge(raw_loaded[r], 16 * (n // SLOTS + 1) if count is None else count)
                if not isinstance(n, int) or n >= SLOTS:
                    act.wait_ge(half_used, n - (SLOTS - 1))
                A(w_hi[r][:, :], raw[r][:, :], ACT.Copy).then_inc(hi_ready, 1)

            for t in range(NT):
                act.wait_ge(x_loaded[t], 16)
                A(y_tok[:, t, :], x_tok[:, t, :], ACT.Square, accum_out=ss_x[:, t:t + 1]).then_inc(sums_x, 1)
            split(0)
            for j in range(4):
                if j == 2:
                    split(1)
                t, kh = divmod(j, 2)
                act.wait_ge(unit_made, unit("h", j) + 1)
                A(h_hi[:, 4 * kh:4 * kh + 4, P * t:P * t + P],
                  ubank(unit("h", j))[:, :].rearrange("p (k s) -> p k s", k=4), ACT.Copy).then_inc(h_hi_ready, 1)
            for n in range(2, SLOTS):
                split(n)
            act.wait_ge(tables_loaded, 48)

            def copy_block(b, dst):
                for t in range(NT):
                    act.wait_ge(half_used, 2 * b + 2)
                    A(dst(t), block_bank(b, t)[:, :], ACT.Copy).then_inc(bank_read[b % 2], 1)

            def head_read(name, dst, gain=None):
                for t in range(NT):
                    u = unit(name, t)
                    act.wait_ge(unit_made, u + 1)
                    A(dst[:, :, P * t:P * t + P], ubank(u)[:, :].rearrange("p (h s) -> p h s", h=4),
                      ACT.Identity, scale=1.0 if gain is None else col[:, gain:gain + 1]).then_inc(unit_read[u % 4], 1)

            def silu_gates(b):
                act.wait_ge(half_used, 2 * b + 2)
                for j in range(2):
                    k = 4 * (b - G_R0) + 2 * j
                    A(g_t[:, k:k + 2, :], block_bank(b, j)[:, :].rearrange("p (m s) -> p m s", m=2), ACT.Silu)\
                        .then_inc(bank_read[b % 2], 1)

            def square_heads(b):
                act.wait_ge(half_used, 2 * b + 2)
                if b > Q_M0:
                    act.wait_ge(sums_qk, 2 * (b - Q_M0))
                for t in range(NT):
                    for h in range(4):
                        ins = A(discard[:, 4 * t + h, :], block_bank(b, t)[:, HEAD * h:HEAD * h + HEAD], ACT.Square,
                                accum_out=ss_qk[:, b - Q_M0, 4 * t + h:4 * t + h + 1])
                    ins.then_inc(sums_qk, 1)

            def sigmoid_gates(b, first, bias):
                act.wait_ge(half_used, 2 * b + 2)
                for j in range(2):
                    if first == GATE_M0:
                        wait_bank_read(act, RET_O1, 1)
                    for i in range(2):
                        k = 4 * (b - first) + 2 * j + i
                        c = COL_GATE_BIAS + bias + k
                        ins = A(gates[:, k, :], block_bank(b, j)[:, SEQ * i:SEQ * i + SEQ], ACT.Sigmoid,
                                bias=col[:, c:c + 1])
                    ins.then_inc(bank_read[b % 2], 1)

            def ret_read():
                for j in range(4):
                    u = unit("ret_t", j)
                    act.wait_ge(unit_made, u + 1)
                    for i in range(2):
                        k = 2 * j + i
                        ins = A(ret_t[:, k, :], ubank(u)[:, SEQ * i:SEQ * i + SEQ], ACT.Identity,
                                scale=col[:, COL_RET_GAIN + k:COL_RET_GAIN + k + 1],
                                bias=col[:, COL_RET_BIAS + k:COL_RET_BIAS + k + 1])
                    ins.then_inc(unit_read[u % 4], 1)
                for j in range(4):
                    act.wait_ge(ret_gated, j + 1)
                    A(a_hi[:, 2 * j:2 * j + 2, :], ret_t[:, 2 * j:2 * j + 2, :], ACT.Copy).then_inc(ret_hi_ready, 1)

            def exps(g):
                act.wait_ge(neg_max_ready, g + 1)
                for j in range(4):
                    for c, (lo_c, hi_c) in enumerate(((0, P), (P, P + SEQ))):
                        i = 8 * g + 2 * j + c
                        ins = A(probs[g][:, j, lo_c:hi_c], probs[g][:, j, lo_c:hi_c], ACT.Exp, scale=QK_SCALE,
                                bias=neg_max[:, i:i + 1], accum_out=row_sum[:, i:i + 1])
                ins.then_inc(exp_done, 1)

            def probs_read(g):
                for j in range(4):
                    u = unit(f"probs{g}", j)
                    act.wait_ge(unit_made, u + 1)
                    A(probs_t[:, 4 * g + j, :], ubank(u)[:, 0:3 * P], ACT.Copy).then_inc(unit_read[u % 4], 1)

            def attn_read(g):
                for j in range(2):
                    u = unit(f"moba_out{g}", j)
                    k = KT + 4 * g + 2 * j
                    act.wait_ge(unit_made, u + 1)
                    A(a_hi[:, k:k + 2, :], ubank(u)[:, :].rearrange("p (m s) -> p m s", m=2), ACT.Copy)\
                        .then_inc(attn_hi_ready, 1)

            def merged_high(b):
                for j in range(2):
                    i = 2 * (b - MOBA_O0) + j
                    act.wait_ge(merged_ready, i + 1)
                    A(h_hi[:, 2 * i:2 * i + 2, :], merged[:, 2 * i:2 * i + 2, :], ACT.Copy).then_inc(merged_hi_ready, 1)

            def square_x2(b):
                for t in range(NT):
                    c = 512 * (b - OUT0)
                    wait_bank_read(act, b, t)
                    A(y_tok[:, t, c:c + 512], x_tok[:, t, c:c + 512], ACT.Square,
                      accum_out=ss_x2[:, 2 * (b - OUT0) + t:2 * (b - OUT0) + t + 1]).then_inc(sums_x2, 1)

            def h2_high():
                for j in range(4):
                    t, kh = divmod(j, 2)
                    u = unit("h2", j)
                    act.wait_ge(unit_made, u + 1)
                    A(h_hi[:, 4 * kh:4 * kh + 4, P * t:P * t + P],
                      ubank(u)[:, :].rearrange("p (k s) -> p k s", k=4), ACT.Copy).then_inc(h2_hi_ready, 1)

            first = {
                K_R: lambda: None,
                V_R0: lambda: copy_block(V_R0, lambda t: v_r[:, t, 0:512]),
                V_R1: lambda: copy_block(V_R1, lambda t: v_r[:, t, 512:1024]),
                G_R0: lambda: silu_gates(G_R0), G_R1: lambda: silu_gates(G_R1),
                Q_M0: lambda: square_heads(Q_M0), Q_M1: lambda: square_heads(Q_M1),
                K_M0: lambda: square_heads(K_M0), K_M1: lambda: square_heads(K_M1),
                V_M0: lambda: copy_block(V_M0, lambda t: v_m[:, t, 0:512]),
                V_M1: lambda: copy_block(V_M1, lambda t: v_m[:, t, 512:1024]),
                GATE_R0: lambda: exps(1),
                GATE_R1: lambda: sigmoid_gates(GATE_R1, GATE_R0, 0),
                RET_O0: lambda: (attn_read(0), probs_read(1)), RET_O1: lambda: attn_read(1),
                GATE_M0: lambda: sigmoid_gates(GATE_M0, GATE_M0, KT),
                GATE_M1: lambda: sigmoid_gates(GATE_M1, GATE_M0, KT),
                MOBA_O0: lambda: merged_high(MOBA_O0), MOBA_O1: lambda: merged_high(MOBA_O1),
                OUT0: lambda: square_x2(OUT0), OUT1: lambda: (square_x2(OUT1), h2_high()),
            }
            second = {
                K_R: lambda: head_read("q_r", qr_t), V_R0: lambda: head_read("k_r", kr_t),
                Q_M1: lambda: head_read("q_m0", qm_t[:, 0:4], COL_Q_GAIN),
                K_M0: lambda: (head_read("q_m1", qm_t[:, 4:8], COL_Q_GAIN), ret_read()),
                K_M1: lambda: head_read("k_m0", km_t[:, 0:4], COL_K_GAIN),
                V_M0: lambda: head_read("k_m1", km_t[:, 4:8], COL_K_GAIN),
                V_M1: lambda: exps(0),
                GATE_R0: lambda: sigmoid_gates(GATE_R0, GATE_R0, 0),
                GATE_R1: lambda: probs_read(0),
            }
            for b in range(UP0):
                first.get(b, lambda: None)()
                split(2 * b + 4)
                second.get(b, lambda: None)()
                split(2 * b + 5)

            def up_read(jj, used, conv_before, read, conv_col):
                act.wait_ge(half_used, used)
                if conv_before is not None:
                    act.wait_ge(a_split, conv_before)
                for j in range(2):
                    A(u_in[:, jj, 2 * j:2 * j + 2, PAD:PAD + SEQ],
                      bank[2 * jj + j][:, :].rearrange("p (m s) -> p m s", m=2), ACT.Copy)
                    for i in range(2):
                        m = 2 * j + i
                        ins = A(conv[:, jj, m, :], bank[2 * jj + j][:, SEQ * i:SEQ * i + SEQ], ACT.Identity,
                                scale=conv_col(4 * m + 2), bias=conv_col(4 * m + 3))
                    ins.then_inc(bank_read[jj], 1)
                act.wait_ge(conv_gate_done, read)
                A(conv[:, jj, 0:2, :], conv[:, jj, 0:2, :], ACT.Silu).then_inc(silu_done, 1)

            def up_high(jj, k, ready):
                act.wait_ge(prod_ready, ready)
                A(a_hi[:, k, :], prod[:, jj, :, :], ACT.Copy).then_inc(a_hi_ready, 1)

            with act.Fori(0, UP_BLOCKS // 2) as i:
                for jj in range(2):
                    up_read(jj, i * 4 + (2 * UP0 + 2 * jj + 2), i * 2 + jj - 1 if jj else i * 2,
                            i * 2 + (jj + 1), lambda c: col[:, bass.ds(i * 32 + (COL_CONV + 16 * jj + c), 1)])
                    r = 2 * jj
                    split(i * 4 + (2 * UP0 + 4 + r), r, i * 16 + 16 * ((2 * UP0 + 4) // SLOTS + 1))
                    up_high(jj, bass.ds(i * 4 + 2 * jj, 2), i * 2 + (jj + 1))
                    r = 2 * jj + 1
                    split(i * 4 + (2 * UP0 + 4 + r), r, i * 16 + 16 * ((2 * UP0 + 4) // SLOTS + 1))
            b = UP_BLOCKS - 1
            up_read(0, DOWN_FIRST_HALF, b, b + 1,
                    lambda c: col[:, COL_CONV + 16 * b + c:COL_CONV + 16 * b + c + 1])
            up_high(0, slice(2 * b, 2 * b + 2), b + 1)
            for n in range(DOWN_FIRST_HALF + 2, HALVES):
                split(n)

        @block.vector
        def _(dve):
            tt = nc.vector.tensor_tensor
            ts = nc.vector.tensor_scalar
            stt = nc.vector.scalar_tensor_tensor
            done = [0]

            def step(ins):
                done[0] += 1
                ins.then_inc(dve_step, 1)
                dve.wait_ge(dve_step, done[0])

            def split(n, r=None):
                r = n % SLOTS if r is None else r
                dve.wait_ge(hi_ready, n + 1)
                tt(w_lo[r][:, :], raw[r][:, :], w_hi[r][:, :].bitcast(f32), ALU.subtract).then_inc(lo_ready, 1)

            dve.wait_ge(gain_loaded, 16)
            for t in range(NT):
                dve.wait_ge(inv_x_ready, t + 1)
                for c in range(2):
                    stt(out=y_tok[:, t, 512 * c:512 * c + 512], in0=x_tok[:, t, 512 * c:512 * c + 512],
                        scalar=inv_x[:, t:t + 1], in1=gain_row[:, 512 * c:512 * c + 512],
                        op0=ALU.mult, op1=ALU.mult).then_inc(xn_ready, 1)
            split(0)
            for j in range(4):
                if j == 2:
                    split(1)
                t, kh = divmod(j, 2)
                u = unit("h", j)
                dve.wait_ge(h_hi_ready, j + 1)
                part = (slice(None), slice(4 * kh, 4 * kh + 4), slice(P * t, P * t + P))
                tt(h_lo[part], ubank(u)[:, :].rearrange("p (k s) -> p k s", k=4), h_hi[part].bitcast(f32),
                   ALU.subtract).then_inc(unit_read[u % 4], 1)
            for n in range(2, SLOTS):
                split(n)
            dve.wait_ge(rotary_loaded, 16)
            dve.wait_ge(tables_loaded, 48)

            def rotate(b):
                dve.wait_ge(half_used, 2 * b + 2)
                tmp = xs[:, 0:512].rearrange("p (h d) -> p h d", h=4)
                for t in range(NT):
                    ps = block_bank(b, t)[:, :].rearrange("p (h d) -> p h d", h=4)
                    dst = rot[:, b, t].rearrange("p (h d) -> p h d", h=4)
                    tt(dst, ps, cos_t[:, t, :].unsqueeze(1).broadcast_to([P, 4, HEAD]), ALU.mult)
                    tt(tmp[:, :, 0:64], ps[:, :, 64:128], sin_t[:, t, 0:64].unsqueeze(1).broadcast_to([P, 4, 64]),
                       ALU.mult)
                    tt(tmp[:, :, 64:128], ps[:, :, 0:64], sin_t[:, t, 64:128].unsqueeze(1).broadcast_to([P, 4, 64]),
                       ALU.mult).then_inc(bank_read[b % 2], 1)
                    wait_bank_read(dve, b, t)
                    tt(dst, dst, tmp, ALU.add).then_inc(rot_ready, 1)
                    dve.wait_ge(rot_ready, 2 * b + t + 1)

            def decays():
                for h in range(RET_HEADS):
                    u = unit("ret_scores", h)
                    dve.wait_ge(unit_made, u + 1)
                    tt(ret_probs[:, h, :], ubank(u)[:, 0:3 * P], decay[:, 3 * P * h:3 * P * h + 3 * P], ALU.mult)\
                        .then_inc(unit_read[u % 4], 1)

            def group_stats():
                for h in range(RET_HEADS):
                    dve.wait_ge(unit_made, unit("ret_out", h) + 1)
                    for t in range(NT):
                        ins = nc.vector.bn_stats(gn_stats[:, 2 * h + t, :],
                                                 ubank(unit("ret_out", h))[:, RET_V * t:RET_V * t + RET_V])
                step(ins)
                for i in range(8):
                    ins = nc.vector.bn_aggr(gn_mv[:, i, :], gn_stats[:, i, :])
                ins.then_inc(gn_stats_ready, 1)
                dve.wait_ge(gn_stats_ready, 1)

            def group_norm():
                dve.wait_ge(gn_rstd_ready, 1)
                for h in range(RET_HEADS):
                    u = unit("ret_out", h)
                    for t in range(NT):
                        i = 2 * h + t
                        ins = ts(y_tok[:, t, RET_V * h:RET_V * h + RET_V], ubank(u)[:, RET_V * t:RET_V * t + RET_V],
                                 gn_mv[:, i, 0:1], gn_rstd[:, i:i + 1], ALU.subtract, ALU.mult)
                    ins.then_inc(unit_read[u % 4], 1)

            def qk_norm(b):
                q = b - Q_M0
                dve.wait_ge(inv_qk_ready, q + 1)
                if q >= 2:
                    dve.wait_ge(unit_made, unit(f"q_m{q - 2}", 1) + 1)
                for t in range(NT):
                    tt(qn[:, q % 2, t].rearrange("p (h d) -> p h d", h=4),
                       block_bank(b, t)[:, :].rearrange("p (h d) -> p h d", h=4),
                       inv_qk[:, q, 4 * t:4 * t + 4].unsqueeze(2).broadcast_to([P, 4, HEAD]), ALU.mult)\
                        .then_inc(bank_read[b % 2], 1)

            def ret_gate():
                for j in range(4):
                    u = unit("ret_t", j)
                    wait_unit_read(dve, u)
                    k = slice(2 * j, 2 * j + 2)
                    tt(ret_t[:, k, :], ret_t[:, k, :], g_t[:, k, :], ALU.mult).then_inc(ret_gated, 1)

            def ret_low():
                for j in range(4):
                    k = slice(2 * j, 2 * j + 2)
                    dve.wait_ge(ret_hi_ready, j + 1)
                    tt(a_lo[:, k, :], ret_t[:, k, :], a_hi[:, k, :].bitcast(f32), ALU.subtract).then_inc(ret_split, 1)

            def masked_max(g):
                for j in range(4):
                    u = unit(f"scores{g}", j)
                    dve.wait_ge(unit_made, u + 1)
                    for c, (lo_c, hi_c) in enumerate(((0, P), (P, P + SEQ))):
                        i = 8 * g + 2 * j + c
                        ins = nc.vector.tensor_tensor_reduce(
                            out=probs[g][:, j, lo_c:hi_c], in0=ubank(u)[:, lo_c:hi_c],
                            in1=mask[:, 2 * P - (hi_c - lo_c):2 * P], scale=1.0, scalar=MASKED,
                            op0=ALU.add, op1=ALU.max, accum_out=row_max[:, i:i + 1])
                    ins.then_inc(unit_read[u % 4], 1)
                wait_unit_read(dve, unit(f"scores{g}", 3))
                ts(neg_max[:, 8 * g:8 * g + 8], row_max[:, 8 * g:8 * g + 8], -QK_SCALE, None, ALU.mult)\
                    .then_inc(neg_max_ready, 1)

            def normalise_probs(g):
                dve.wait_ge(exp_done, g + 1)
                step(nc.vector.reciprocal(inv_sum[:, 8 * g:8 * g + 8], row_sum[:, 8 * g:8 * g + 8]))
                for j in range(4):
                    for c, (lo_c, hi_c) in enumerate(((0, P), (P, P + SEQ))):
                        i = 8 * g + 2 * j + c
                        ins = ts(probs[g][:, j, lo_c:hi_c], probs[g][:, j, lo_c:hi_c], inv_sum[:, i:i + 1], None,
                                 ALU.mult)
                    ins.then_inc(probs_ready, 1)

            def attn_low(g):
                for j in range(2):
                    u = unit(f"moba_out{g}", j)
                    k = slice(KT + 4 * g + 2 * j, KT + 4 * g + 2 * j + 2)
                    dve.wait_ge(attn_hi_ready, 2 * g + j + 1)
                    tt(a_lo[:, k, :], ubank(u)[:, :].rearrange("p (m s) -> p m s", m=2), a_hi[:, k, :].bitcast(f32),
                       ALU.subtract).then_inc(unit_read[u % 4], 1)

            def gate_ret(b):
                dve.wait_ge(half_used, 2 * b + 2)
                if b == RET_O0:
                    dve.wait_ge(unit_made, unit("probs1", 3) + 1)
                    wait_bank_read(dve, GATE_R0, 1)
                    wait_bank_read(dve, GATE_R1, 1)
                for j in range(2):
                    k = slice(4 * (b - RET_O0) + 2 * j, 4 * (b - RET_O0) + 2 * j + 2)
                    tt(merged[:, k, :], block_bank(b, j)[:, :].rearrange("p (m s) -> p m s", m=2), gates[:, k, :],
                       ALU.mult).then_inc(bank_read[b % 2], 1)
                wait_bank_read(dve, b, 1)

            def gate_moba(b):
                dve.wait_ge(half_used, 2 * b + 2)
                if b == MOBA_O0:
                    wait_bank_read(dve, GATE_M0, 1)
                    wait_bank_read(dve, GATE_M1, 1)
                for j in range(2):
                    i = 2 * (b - MOBA_O0) + j
                    k = slice(2 * i, 2 * i + 2)
                    tt(gates[:, k, :], block_bank(b, j)[:, :].rearrange("p (m s) -> p m s", m=2), gates[:, k, :],
                       ALU.mult).then_inc(bank_read[b % 2], 1)
                    wait_bank_read(dve, b, j)
                    tt(merged[:, k, :], merged[:, k, :], gates[:, k, :], ALU.add).then_inc(merged_ready, 1)
                for j in range(2):
                    i = 2 * (b - MOBA_O0) + j
                    k = slice(2 * i, 2 * i + 2)
                    dve.wait_ge(merged_hi_ready, i + 1)
                    tt(h_lo[:, k, :], merged[:, k, :], h_hi[:, k, :].bitcast(f32), ALU.subtract)\
                        .then_inc(merged_split, 1)

            def residual(b):
                for t in range(NT):
                    if b == OUT0:
                        dve.wait_ge(half_used, 2 * OUT0 + 3)
                        dve.wait_ge(x_again, 16)
                    elif t == 0:
                        dve.wait_ge(out_chunk0, 1)
                    else:
                        dve.wait_ge(half_used, 2 * OUT0 + 4)
                    c = 512 * (b - OUT0)
                    tt(x_tok[:, t, c:c + 512], block_bank(b, t)[:, :], x_tok[:, t, c:c + 512], ALU.add)\
                        .then_inc(bank_read[b % 2], 1)

            def norm2():
                dve.wait_ge(gain2_loaded, 16)
                for t in range(NT):
                    dve.wait_ge(inv_x2_ready, t + 1)
                    for c in range(2):
                        stt(out=y_tok[:, t, 512 * c:512 * c + 512], in0=x_tok[:, t, 512 * c:512 * c + 512],
                            scalar=inv_x2[:, t:t + 1], in1=gain_row[:, 512 * c:512 * c + 512],
                            op0=ALU.mult, op1=ALU.mult).then_inc(xn2_ready, 1)
                nc.vector.memset(u_in[:, 0, :, 0:PAD], 0.0)
                nc.vector.memset(u_in[:, 1, :, 0:PAD], 0.0).then_inc(pads_zero, 1)
                dve.wait_ge(pads_zero, 1)
                for j in range(4):
                    t, kh = divmod(j, 2)
                    u = unit("h2", j)
                    dve.wait_ge(h2_hi_ready, j + 1)
                    part = (slice(None), slice(4 * kh, 4 * kh + 4), slice(P * t, P * t + P))
                    tt(h_lo[part], ubank(u)[:, :].rearrange("p (k s) -> p k s", k=4), h_hi[part].bitcast(f32),
                       ALU.subtract).then_inc(unit_read[u % 4], 1)

            first = {
                Q_R: lambda: rotate(Q_R), K_R: lambda: rotate(K_R),
                V_R1: decays, G_R0: group_stats,
                V_M1: lambda: masked_max(0), GATE_R0: lambda: masked_max(1),
                RET_O0: lambda: attn_low(0), RET_O1: lambda: (gate_ret(RET_O1), attn_low(1)),
                MOBA_O0: lambda: gate_moba(MOBA_O0), MOBA_O1: lambda: gate_moba(MOBA_O1),
                OUT0: lambda: residual(OUT0), OUT1: lambda: (residual(OUT1), norm2()),
            }
            second = {
                G_R0: group_norm,
                Q_M0: lambda: qk_norm(Q_M0), Q_M1: lambda: qk_norm(Q_M1), K_M0: lambda: (qk_norm(K_M0), ret_gate()),
                K_M1: lambda: (qk_norm(K_M1), ret_low()),
                V_M1: lambda: normalise_probs(0), GATE_R0: lambda: normalise_probs(1),
                RET_O0: lambda: gate_ret(RET_O0),
            }
            for b in range(UP0):
                first.get(b, lambda: None)()
                split(2 * b + 4)
                second.get(b, lambda: None)()
                split(2 * b + 5)

            def up_conv(jj, read, silu, conv_col, conv_steps):
                for j in range(2):
                    dve.wait_ge(bank_read[jj], read(j))
                    for tap in (1, 0):
                        for i in range(2):
                            m = 2 * j + i
                            ins = stt(out=conv[:, jj, m, :], in0=u_in[:, jj, m, tap:tap + SEQ],
                                      scalar=conv_col(4 * m + tap), in1=conv[:, jj, m, :], op0=ALU.mult, op1=ALU.add)
                        if tap or j:
                            ins.then_inc(dve_step, 1)
                            dve.wait_ge(dve_step, conv_steps(2 * j + 1 - tap if j else 0))
                        else:
                            ins.then_inc(conv_gate_done, 1)
                dve.wait_ge(silu_done, silu)
                tt(prod[:, jj, :, :], conv[:, jj, 0:2, :], conv[:, jj, 2:4, :], ALU.mult).then_inc(prod_ready, 1)

            def up_low(jj, k, ready):
                dve.wait_ge(a_hi_ready, ready)
                tt(a_lo[:, k, :], prod[:, jj, :, :], a_hi[:, k, :].bitcast(f32), ALU.subtract).then_inc(a_split, 1)

            steps0 = done[0]
            order = {0: 1, 2: 2, 3: 3}
            with dve.Fori(0, UP_BLOCKS // 2) as i:
                for jj in range(2):
                    up_conv(jj, lambda j: i * 2 + (UP0 + j + 1), i * 2 + (jj + 1),
                            lambda c: col[:, bass.ds(i * 32 + (COL_CONV + 16 * jj + c), 1)],
                            lambda s: i * 6 + (steps0 + 3 * jj + order[s]))
                    r = 2 * jj
                    split(i * 4 + (2 * UP0 + 4 + r), r)
                    up_low(jj, bass.ds(i * 4 + 2 * jj, 2), i * 2 + (jj + 1))
                    r = 2 * jj + 1
                    split(i * 4 + (2 * UP0 + 4 + r), r)
            b = UP_BLOCKS - 1
            up_conv(0, lambda j: UP0 + b + j + 1, b + 1,
                    lambda c: col[:, COL_CONV + 16 * b + c:COL_CONV + 16 * b + c + 1],
                    lambda s: steps0 + 3 * b + order[s])
            up_low(0, slice(2 * b, 2 * b + 2), b + 1)
            for n in range(DOWN_FIRST_HALF + 2, HALVES):
                split(n)
            for t in range(NT):
                if t == 0:
                    dve.wait_ge(down_chunk0, 1)
                else:
                    dve.wait_ge(half_used, HALVES)
                for c in range(2):
                    tt(y_tok[:, t, 512 * c:512 * c + 512], bank[4 + 2 * t + c][:, :],
                       x_tok[:, t, 512 * c:512 * c + 512], ALU.add).then_inc(out_ready, 1)


def _block_halves(w, columns):
    m = w[:, columns].reshape(2, 4, P, BLOCK_COLS).transpose(0, 2, 1, 3)
    return [m[0].reshape(P, HALF_ELEMS), m[1].reshape(P, HALF_ELEMS)]


def _columns(v):
    return v.reshape(-1, P).T


def _pack_weights(w_in, w_gate, w_ret_o, w_moba_o, w_out, w_up, w_down):
    halves = []
    cut = [slice(BLOCK_COLS * i, BLOCK_COLS * (i + 1)) for i in range(12)]
    for i in range(12):
        halves += _block_halves(w_in, cut[i])
    for w, i in ((w_gate, 0), (w_gate, 1), (w_ret_o, 0), (w_ret_o, 1), (w_gate, 2), (w_gate, 3),
                 (w_moba_o, 0), (w_moba_o, 1)):
        halves += _block_halves(w, cut[i])
    o0, o1 = (_block_halves(w_out, cut[i]) for i in range(2))
    halves += [o0[0], o1[0], o0[1], o1[1]]
    for j in range(UP_BLOCKS):
        c = np.r_[UP_COLS * j:UP_COLS * (j + 1), D_FF + UP_COLS * j:D_FF + UP_COLS * (j + 1)]
        halves += _block_halves(w_up, c)
    down = w_down.reshape(DOWN_HALVES, 2, P, D).transpose(0, 2, 1, 3).reshape(DOWN_HALVES, P, HALF_ELEMS)
    return np.ascontiguousarray(np.concatenate([np.stack(halves), down]))


def _tables():
    half = RET_QK // 2
    inv_freq = np.power(np.float32(10000.0), -np.arange(half, dtype=np.float32) / np.float32(half))
    ang = (np.arange(SEQ, dtype=np.float32)[:, None] * inv_freq[None, :].astype(np.float32)).astype(np.float64)
    cos, sin = np.cos(ang), np.sin(ang)
    cos2 = np.concatenate([cos, cos], 1).reshape(NT, P, RET_QK).transpose(1, 0, 2).reshape(P, -1)
    sin2 = np.concatenate([-sin, sin], 1).reshape(NT, P, RET_QK).transpose(1, 0, 2).reshape(P, -1)
    rotary = np.concatenate([cos2, sin2], 1).astype(np.float32)
    key, query = np.arange(P)[:, None], np.arange(SEQ)[None, :]
    decay = np.zeros((P, RET_HEADS, 3 * P))
    for h in range(RET_HEADS):
        d = np.where(query >= key, np.exp(np.log1p(-2.0 ** (-5.0 - h)) * np.maximum(query - key, 0)), 0.0)
        decay[:, h, 0:SEQ] = d
        decay[:, h, SEQ:] = d[:, 0:P]
    decay = (decay * RET_QK ** -0.5).reshape(P, -1).astype(np.float32)
    mask = np.zeros((P, 2 * P), np.float32)
    mask[:, P:] = np.where(np.arange(P)[None, :] <= np.arange(P)[:, None], 0.0, MASKED)
    return rotary, decay, mask, np.eye(P, dtype=np.float32)


def kernel(x, attn_norm, w_in, ret_norm_gain, ret_norm_bias, moba_q_gain, moba_k_gain, w_ret_o, w_moba_o,
           w_gate, b_gate, w_out, ffn_norm, w_up, conv_w, conv_b, w_down):
    import concourse.bacc as bacc
    from concourse.bass_utils import run_bass_kernel_spmd

    a = {k: np.asarray(v) for k, v in locals().items() if k not in ("bacc", "run_bass_kernel_spmd")}
    taps = np.concatenate([a["conv_w"][0], a["conv_b"][0][None]]).reshape(4, 2, UP_BLOCKS, 2, P)
    conv_cols = taps.transpose(4, 2, 1, 3, 0).reshape(P, CONV_COLS)
    rotary, decay, mask, eye = _tables()
    arrays = {
        "x": a["x"][0],
        "weights": _pack_weights(*(a[n][0] for n in ("w_in", "w_gate", "w_ret_o", "w_moba_o", "w_out", "w_up",
                                                     "w_down"))),
        "gain_rows": np.stack([a["attn_norm"][0], a["ffn_norm"][0]]),
        "cols": np.concatenate([_columns(a["moba_q_gain"][0]), _columns(a["moba_k_gain"][0]),
                                _columns(a["ret_norm_gain"][0]), _columns(a["ret_norm_bias"][0]),
                                _columns(a["b_gate"][0]), conv_cols], 1),
        "ident": eye, "mask": mask, "rotary": rotary, "decay": decay,
    }
    nc = bacc.Bacc("TRN2", target_bir_lowering=False, num_devices=1)
    arrays = {f"{k}_dram": np.ascontiguousarray(v) for k, v in arrays.items()}
    args = [nc.dram_tensor(k, v.shape, mybir.dt.from_np(v.dtype), kind="ExternalInput").ap()
            for k, v in arrays.items()]
    out = nc.dram_tensor("out_dram", (SEQ, D), mybir.dt.float32, kind="ExternalOutput").ap()
    hybrid_layer(nc, *args, out)
    r = run_bass_kernel_spmd(nc, [arrays], core_ids=[0])
    return r.results[0]["out_dram"].reshape(1, SEQ, D)
```

```python
import math

import numpy as np

import concourse.bass as bass
from concourse import mybir
from contextlib import ExitStack

P = 128
SEQ, D = 256, 1024
NT = SEQ // P
KT = D // P
RET_HEADS, RET_QK, RET_V = 4, 128, 256
MOBA_HEADS, HEAD = 8, 128
D_FF = 2816
EPS = 1e-6
BLOCK_COLS = 512
HALF_ELEMS = 2048
SLOTS = 4
UP_COLS = 256
UP_BLOCKS = D_FF // UP_COLS
DOWN_HALVES = D_FF // P // 2
WARM_UP = 17, 6
QK_SCALE = 1.0 / math.sqrt(HEAD)
MASKED = -3.0e38

(V_R0, V_R1, Q_R, K_R, G_R0, G_R1, Q_M0, Q_M1, K_M0, K_M1, V_M0, V_M1,
 GATE_R0, GATE_R1, RET_O0, RET_O1, GATE_M0, GATE_M1, MOBA_O0, MOBA_O1,
 OUT0, OUT1, UP0) = range(23)
DOWN_FIRST_HALF = 2 * (UP0 + UP_BLOCKS)
HALVES = DOWN_FIRST_HALF + DOWN_HALVES

UNITS = {}
for _name, _count in (("h", 4), ("ret_scores", 4), ("ret_out", 4), ("q_m0", 2), ("ret_t0", 2),
                      ("q_m1", 2), ("ret_t1", 2), ("k_m0", 2), ("k_m1", 2), ("scores0", 4), ("scores1", 4),
                      ("probs0", 4), ("moba_out0", 2), ("probs1", 4), ("moba_out1", 2), ("h2", 4)):
    UNITS[_name] = (sum(c for _, c in UNITS.values()), _count)


def unit(name, j):
    return UNITS[name][0] + j


COL_Q_GAIN, COL_K_GAIN, COL_RET_GAIN, COL_RET_BIAS, COL_GATE_BIAS, COL_CONV = 0, 1, 2, 10, 18, 34
CONV_COLS = 16 * UP_BLOCKS
COLS = COL_CONV + CONV_COLS


def hybrid_layer(nc, x, weights, gain_rows, cols, ident_in, mask_in, rotary_in, decay_in, out):
    f32 = mybir.dt.float32
    f32r = mybir.dt.float32r
    ALU = mybir.AluOpType
    ACT = mybir.ActivationFunctionType

    x_view = x.rearrange("(t p) d -> p t d", p=P)
    out_view = out.rearrange("(t p) d -> p t d", p=P)

    with ExitStack() as ctx:
        def sb(name, shape, dt=f32):
            return ctx.enter_context(nc.sbuf_tensor(name, shape, dt))

        def sem(name):
            return ctx.enter_context(nc.semaphore(name))

        raw = [sb(f"w_raw{r}", [P, HALF_ELEMS]) for r in range(SLOTS)]
        w_hi = [sb(f"w_hi{r}", [P, HALF_ELEMS], f32r) for r in range(SLOTS)]
        w_lo = [sb(f"w_lo{r}", [P, HALF_ELEMS], f32r) for r in range(SLOTS)]
        h_hi = sb("h_hi", [P, KT, SEQ], f32r)
        h_lo = sb("h_lo", [P, KT, SEQ], f32r)
        a_hi = sb("a_hi", [P, D_FF // P, SEQ], f32r)
        a_lo = sb("a_lo", [P, D_FF // P, SEQ], f32r)
        area = sb("area", [P, 8192])
        xs = sb("xs", [P, 2048])
        ys = sb("ys", [P, 2048])
        ident = sb("ident", [P, P])
        mask = sb("mask", [P, 2 * P])
        col = sb("col", [P, COLS])
        ss_x = sb("ss_x", [P, 2])
        inv_x = sb("inv_x", [P, 2])
        ss_qk = sb("ss_qk", [P, 4, 8])
        inv_qk = sb("inv_qk", [P, 4, 8])
        gn_stats = sb("gn_stats", [P, 8, 6])
        gn_mv = sb("gn_mv", [P, 8, 2])
        gn_rstd = sb("gn_rstd", [P, 8])
        neg_half = sb("neg_half", [P, 8])
        row_max = sb("row_max", [P, 16])
        neg_max = sb("neg_max", [P, 16])
        row_sum = sb("row_sum", [P, 16])
        inv_sum = sb("inv_sum", [P, 16])
        ss_x2 = sb("ss_x2", [P, 4])
        inv_x2 = sb("inv_x2", [P, 2])

        cos_t = area[:, 0:256]
        sin_t = area[:, 256:512]
        rotary = area[:, 0:512]
        decay = area[:, 512:2048]
        ret_t = area[:, 0:2048].rearrange("p (k s) -> p k s", k=KT)
        gates = area[:, 0:2048].rearrange("p (k s) -> p k s", k=KT)
        qr_t = area[:, 2048:3072].rearrange("p (h s) -> p h s", h=RET_HEADS)
        kr_t = area[:, 3072:4096].rearrange("p (h s) -> p h s", h=RET_HEADS)
        v_r = area[:, 4096:6144].rearrange("p (t d) -> p t d", t=NT)
        qm_t = area[:, 2048:4096].rearrange("p (h s) -> p h s", h=MOBA_HEADS)
        km_t = area[:, 4096:6144].rearrange("p (h s) -> p h s", h=MOBA_HEADS)
        g_t = area[:, 6144:8192].rearrange("p (k s) -> p k s", k=KT)
        v_m = area[:, 6144:8192].rearrange("p (t d) -> p t d", t=NT)
        probs_t = area[:, 2048:5120].rearrange("p (h s) -> p h s", h=MOBA_HEADS)
        gain_row = area[:, 5120:6144]
        PAD = 2
        u_in = area[:, 0:2 * 4 * (PAD + SEQ)].rearrange("p (b m s) -> p b m s", b=2, m=4)
        conv = area[:, 2064:2064 + 2048].rearrange("p (b m s) -> p b m s", b=2, m=4)
        discard = a_hi[:, 2 * KT:2 * KT + 4, :].rearrange("p k (i c) -> p (k i) c", c=P)
        prod = area[:, 6144:7168].rearrange("p (b m s) -> p b m s", b=2, m=2)
        x_tok = xs[:, :].rearrange("p (t d) -> p t d", t=NT)
        y_tok = ys[:, :].rearrange("p (t d) -> p t d", t=NT)
        qn = xs[:, :].rearrange("p (b t d) -> p b t d", b=2, t=NT)
        ret_probs = xs[:, 0:1536].rearrange("p (h s) -> p h s", h=4)
        probs = [xs[:, 0:1536].rearrange("p (h s) -> p h s", h=4),
                 ys[:, 0:1536].rearrange("p (h s) -> p h s", h=4)]
        merged = ys[:, :].rearrange("p (k s) -> p k s", k=KT)

        bank = [ctx.enter_context(nc.psum_tensor(f"bank{i}", [P, 512], f32)) for i in range(8)]

        raw_loaded = [sem(f"raw_loaded{r}") for r in range(SLOTS)]
        raw_start = sem("raw_start")
        hi_ready = sem("hi_ready")
        lo_ready = sem("lo_ready")
        piece_hi = sem("piece_hi")
        piece_lo = sem("piece_lo")
        half_used = sem("half_used")
        bank_read = [sem(f"bank_read{s}") for s in range(2)]
        unit_made = sem("unit_made")
        unit_read = [sem(f"unit_read{k}") for k in range(4)]
        x_loaded = [sem(f"x_loaded{t}") for t in range(NT)]
        gain_loaded = sem("gain_loaded")
        ident_loaded = sem("ident_loaded")
        rotary_loaded = sem("rotary_loaded")
        tables_loaded = sem("tables_loaded")
        x_again = sem("x_again")
        gain2_loaded = sem("gain2_loaded")
        zeros_ready = sem("zeros_ready")
        sums_x = [sem(f"sums_x{t}") for t in range(NT)]
        inv_x_ready = sem("inv_x_ready")
        xn_ready = sem("xn_ready")
        h_hi_ready = sem("h_hi_ready")
        rot_ready = sem("rot_ready")
        gn_stats_ready = sem("gn_stats_ready")
        gn_rstd_ready = sem("gn_rstd_ready")
        sums_qk = sem("sums_qk")
        inv_qk_ready = sem("inv_qk_ready")
        ret_affine = sem("ret_affine")
        ret_gated = sem("ret_gated")
        ret_hi_ready = sem("ret_hi_ready")
        ret_split = sem("ret_split")
        neg_max_ready = sem("neg_max_ready")
        exp_done = sem("exp_done")
        probs_ready = sem("probs_ready")
        attn_hi_ready = sem("attn_hi_ready")
        merged_ready = sem("merged_ready")
        merged_hi_ready = sem("merged_hi_ready")
        merged_split = sem("merged_split")
        out_chunk0 = sem("out_chunk0")
        sums_x2 = sem("sums_x2")
        inv_x2_ready = sem("inv_x2_ready")
        xn2_ready = sem("xn2_ready")
        h2_hi_ready = [sem(f"h2_hi_ready{kh}") for kh in range(2)]
        conv_gate_done = sem("conv_gate_done")
        silu_done = sem("silu_done")
        prod_ready = sem("prod_ready")
        a_hi_ready = sem("a_hi_ready")
        a_split = sem("a_split")
        quarter_summed = sem("quarter_summed")
        out_ready = sem("out_ready")
        stored = sem("stored")
        dve_step = sem("dve_step")
        pool_step = sem("pool_step")

        def ubank(u):
            return bank[4 + u % 4]

        def wait_unit_read(eng, u):
            eng.wait_ge(unit_read[u % 4], u // 4 + 1)

        def wait_bank_read(eng, b, j):
            eng.wait_ge(bank_read[b % 2], 2 * (b // 2) + j + 1)

        def block_bank(b, j):
            return bank[2 * (b % 2) + j]

        block = ctx.enter_context(nc.Block())

        @block.sync
        def _(sp):
            for t in range(NT):
                sp.dma_start(x_tok[:, t, :], x_view[:, t, :]).then_inc(x_loaded[t], 16)
            for c in range(2):
                part = slice(c * HALF_ELEMS // 2, (c + 1) * HALF_ELEMS // 2)
                sp.dma_start(raw[0][:, part], weights[0, :, part]).then_inc(raw_loaded[0] if c else raw_start, 16)
            for r in range(1, SLOTS):
                sp.dma_start(raw[r][:, :], weights[r]).then_inc(raw_loaded[r], 16)
            ROUNDS = (HALVES - SLOTS) // SLOTS
            with sp.Fori(0, ROUNDS) as i:
                for r in range(SLOTS):
                    sp.wait_ge(lo_ready, i * SLOTS + (r + 1))
                    sp.dma_start(raw[r][:, :], weights[i * SLOTS + (r + SLOTS)]).then_inc(raw_loaded[r], 16)
            for n in range(SLOTS * (ROUNDS + 1), HALVES):
                sp.wait_ge(lo_ready, n - SLOTS + 1)
                sp.dma_start(raw[n % SLOTS][:, :], weights[n]).then_inc(raw_loaded[n % SLOTS], 16)
            for t in range(NT):
                for n in range(2):
                    sp.wait_ge(out_ready, 2 * t + n + 1)
                    sp.dma_start(out_view[:, t, 512 * n:512 * n + 512],
                                 y_tok[:, t, 512 * n:512 * n + 512]).then_inc(stored, 16)
            sp.wait_ge(stored, 16 * 4)

        @block.gpsimd
        def _(pool):
            done = [0]

            def step(ins):
                done[0] += 1
                ins.then_inc(pool_step, 1)
                pool.wait_ge(pool_step, done[0])

            def inv_sqrt(dst, src, factor, width):
                step(nc.gpsimd.tensor_scalar(dst, src, factor, EPS, ALU.mult, ALU.add))
                return nc.gpsimd.tensor_tensor(dst, dst, neg_half[:, 0:width], ALU.pow)

            step(nc.gpsimd.memset(neg_half[:, :], -0.5))
            for t in range(NT):
                pool.wait_ge(sums_x[t], 1)
                inv_sqrt(inv_x[:, t:t + 1], ss_x[:, t:t + 1], 1.0 / D, 1).then_inc(inv_x_ready, 1)
            pool.wait_ge(gn_stats_ready, 1)
            inv_sqrt(gn_rstd[:, :], gn_mv[:, :, 1], 1.0, 8).then_inc(gn_rstd_ready, 1)
            for q in range(4):
                pool.wait_ge(sums_qk, 2 * (q + 1))
                inv_sqrt(inv_qk[:, q, :], ss_qk[:, q, :], 1.0 / HEAD, 8).then_inc(inv_qk_ready, 1)
            pool.wait_ge(unit_made, unit("probs0", 3) + 1)
            pool.dma_start(x_tok, x_view).then_inc(x_again, 16)
            pool.dma_start(gain_row, gain_rows[1:2, :].partition_broadcast(P)).then_inc(gain2_loaded, 16)
            pool.wait_ge(sums_x2, 2)
            step(nc.gpsimd.tensor_scalar(inv_x2[:, :], ss_x2[:, 0:NT], 1.0 / D, EPS, ALU.mult, ALU.add))
            for t in range(NT):
                pool.wait_ge(sums_x2, 3 + t)
                step(nc.gpsimd.tensor_scalar(inv_x2[:, t:t + 1], ss_x2[:, NT + t:NT + t + 1], 1.0 / D,
                                             inv_x2[:, t:t + 1], ALU.mult, ALU.add))
                nc.gpsimd.tensor_tensor(inv_x2[:, t:t + 1], inv_x2[:, t:t + 1], neg_half[:, 0:1], ALU.pow)\
                    .then_inc(inv_x2_ready, 1)

        @block.tensor
        def _(pe):
            mm = nc.tensor.matmul

            def wait_bank_free(b):
                if b >= 2:
                    wait_bank_read(pe, b - 2, 1)

            def start_unit(name, j):
                u = unit(name, j)
                if u >= 4:
                    wait_unit_read(pe, u - 4)
                return ubank(u)

            def token_half(out_banks, n, tiles, first, last, order=None, chunk0=None, before=None):
                hi = w_hi[n % SLOTS][:, :].rearrange("p (k c) -> p k c", k=4)
                lo = w_lo[n % SLOTS][:, :].rearrange("p (k c) -> p k c", k=4)
                pairs = order or [(kk, t) for kk in range(4) for t in range(NT)]
                for kk, t in pairs:
                    if before and t == 0:
                        before(kk)
                    k = tiles[kk]
                    s_hi = h_hi[:, k, P * t:P * t + P]
                    s_lo = h_lo[:, k, P * t:P * t + P]
                    o = out_banks[t][:, :]
                    mm(o, s_hi, hi[:, kk, :], start=(first and kk == 0), stop=False)
                    mm(o, s_hi, lo[:, kk, :], start=False, stop=False)
                    ins = mm(o, s_lo, hi[:, kk, :], start=False, stop=(last and kk == 3))
                    if chunk0 is not None and (kk, t) == (3, 0):
                        ins.then_inc(chunk0, 1)
                return ins

            def token_block(b):
                for h in range(2):
                    n = 2 * b + h

                    def quarter_split(kk):
                        if h == 0 and kk == 2:
                            h_transposes(1)
                        if kk < 3:
                            pe.wait_ge(piece_lo, 3 * n + kk + 1)
                        else:
                            pe.wait_ge(lo_ready, n + 1)

                    if b == 0:
                        for t in range(NT):
                            wait_unit_read(pe, unit("h", 2 * h + t))
                    else:
                        pe.wait_ge(lo_ready, n + 1)
                    if h == 0:
                        wait_bank_free(b)
                    token_half([block_bank(b, t) for t in range(NT)], n, range(4 * h, 4 * h + 4), h == 0, h == 1,
                               before=quarter_split if b == 0 else None).then_inc(half_used, 1)

            def channel_half(banks, slot, r_hi, r_lo, h):
                hi = w_hi[slot][:, :].rearrange("p (k c) -> p k c", k=4)
                lo = w_lo[slot][:, :].rearrange("p (k c) -> p k c", k=4)
                for m in range(4):
                    o = banks[m // 2][:, SEQ * (m % 2):SEQ * (m % 2) + SEQ]
                    for kk in range(4):
                        k = 4 * h + kk
                        s_hi, s_lo = hi[:, kk, P * m:P * m + P], lo[:, kk, P * m:P * m + P]
                        mm(o, s_hi, r_hi[:, k, :], start=(k == 0 and m % 2 == 0), stop=False)
                        mm(o, s_hi, r_lo[:, k, :], start=False, stop=False)
                        ins = mm(o, s_lo, r_hi[:, k, :], start=False, stop=(k == KT - 1 and m % 2 == 1))
                return ins

            def channel_block(b, r_hi, r_lo):
                for h in range(2):
                    n = 2 * b + h
                    pe.wait_ge(lo_ready, n + 1)
                    if h == 0:
                        wait_bank_free(b)
                    channel_half([block_bank(b, 0), block_bank(b, 1)], n % SLOTS, r_hi, r_lo, h)\
                        .then_inc(half_used, 1)

            def transposes(name, j, pieces):
                o = start_unit(name, j)
                for c, piece in enumerate(pieces):
                    ins = nc.tensor.transpose(o[:, P * c:P * c + P], piece, ident[:, :])
                ins.then_inc(unit_made, 1)

            def head_transposes(name, b, src):
                for t in range(NT):
                    wait_bank_read(pe, b, t)
                    transposes(name, t, [src[:, t, P * h:P * h + P] for h in range(4)])

            pe.wait_ge(zeros_ready, 1)
            def keep_warm(count):
                for _ in range(count):
                    mm(bank[7][:, :], w_lo[SLOTS - 1][:, 0:P], w_lo[SLOTS - 1][:, 0:512], start=True, stop=True)

            keep_warm(WARM_UP[0])

            pe.wait_ge(ident_loaded, 16)
            def h_transposes(kh):
                for t in range(NT):
                    pe.wait_ge(xn_ready, 2 * kh + t + 1)
                    transposes("h", 2 * kh + t, [y_tok[:, t, P * k:P * k + P] for k in range(4 * kh, 4 * kh + 4)])

            def tail_ret_scores():
                for h in range(RET_HEADS):
                    if h == 0:
                        pe.wait_ge(rot_ready, 4)
                    o = start_unit("ret_scores", h)
                    mm(o[:, 0:SEQ], kr_t[:, h, 0:P], qr_t[:, h, :], start=True, stop=False)
                    mm(o[:, SEQ:SEQ + P], kr_t[:, h, P:SEQ], qr_t[:, h, P:SEQ], start=False, stop=True)\
                        .then_inc(unit_made, 1)

            def tail_ret_out():
                wait_bank_read(pe, V_R0, 1)
                wait_bank_read(pe, V_R1, 1)
                for h in range(RET_HEADS):
                    wait_unit_read(pe, unit("ret_scores", h))
                    o = start_unit("ret_out", h)
                    v0, v1 = (v_r[:, t, RET_V * h:RET_V * h + RET_V] for t in range(NT))
                    mm(o[:, 0:RET_V], ret_probs[:, h, 0:P], v0, start=True, stop=False)
                    mm(o[:, RET_V:2 * RET_V], ret_probs[:, h, P:SEQ], v0, start=False, stop=False)
                    mm(o[:, RET_V:2 * RET_V], ret_probs[:, h, SEQ:SEQ + P], v1, start=False, stop=True)\
                        .then_inc(unit_made, 1)

            def tail_ret_transpose(g):
                for j in range(2):
                    i = 2 * g + j
                    wait_unit_read(pe, unit("ret_out", i))
                    transposes(f"ret_t{g}", j,
                               [y_tok[:, t, P * k:P * k + P] for k in (2 * i, 2 * i + 1) for t in range(NT)])

            def tail_scores(g):
                for j in range(4):
                    h = 4 * g + j
                    if j == 0:
                        for which in ("q_m", "k_m"):
                            wait_unit_read(pe, unit(f"{which}{g}", 1))
                    o = start_unit(f"scores{g}", j)
                    mm(o[:, 0:P], qm_t[:, h, 0:P], km_t[:, h, 0:P], start=True, stop=False)
                    mm(o[:, P:P + SEQ], qm_t[:, h, P:SEQ], km_t[:, h, :], start=False, stop=True)\
                        .then_inc(unit_made, 1)

            def tail_probs(g):
                for j in range(4):
                    pe.wait_ge(probs_ready, 4 * g + j + 1)
                    transposes(f"probs{g}", j, [probs[g][:, j, P * c:P * c + P] for c in range(3)])

            def tail_moba_out(g):
                if g == 0:
                    wait_bank_read(pe, V_M0, 1)
                    wait_bank_read(pe, V_M1, 1)
                for j in range(2):
                    o = start_unit(f"moba_out{g}", j)
                    for i in range(2):
                        h = 4 * g + 2 * j + i
                        wait_unit_read(pe, unit(f"probs{g}", 2 * j + i))
                        v0, v1 = (v_m[:, t, HEAD * h:HEAD * h + HEAD] for t in range(NT))
                        mm(o[:, SEQ * i:SEQ * i + SEQ], v0, probs_t[:, h, 0:SEQ], start=(i == 0), stop=False)
                        ins = mm(o[:, SEQ * i + P:SEQ * i + SEQ], v1, probs_t[:, h, SEQ:SEQ + P],
                                 start=False, stop=(i == 1))
                    ins.then_inc(unit_made, 1)

            h_transposes(0)
            keep_warm(WARM_UP[1])
            token_block(V_R0)
            token_block(V_R1)
            channel_block(Q_R, h_hi, h_lo)
            channel_block(K_R, h_hi, h_lo)
            channel_block(G_R0, h_hi, h_lo)
            tail_ret_scores()
            channel_block(G_R1, h_hi, h_lo)
            tail_ret_out()
            token_block(Q_M0)
            token_block(Q_M1)
            head_transposes("q_m0", Q_M0, qn[:, 0])
            tail_ret_transpose(0)
            token_block(K_M0)
            head_transposes("q_m1", Q_M1, qn[:, 1])
            tail_ret_transpose(1)
            token_block(K_M1)
            head_transposes("k_m0", K_M0, qn[:, 0])
            token_block(V_M0)
            head_transposes("k_m1", K_M1, qn[:, 1])
            token_block(V_M1)
            tail_scores(0)
            channel_block(GATE_R0, h_hi, h_lo)
            tail_scores(1)
            channel_block(GATE_R1, h_hi, h_lo)
            tail_probs(0)
            pe.wait_ge(ret_split, 4)
            channel_block(RET_O0, a_hi, a_lo)
            tail_moba_out(0)
            tail_probs(1)
            channel_block(RET_O1, a_hi, a_lo)
            tail_moba_out(1)
            channel_block(GATE_M0, h_hi, h_lo)
            channel_block(GATE_M1, h_hi, h_lo)
            wait_unit_read(pe, unit("moba_out1", 1))
            channel_block(MOBA_O0, a_hi[:, KT:2 * KT], a_lo[:, KT:2 * KT])
            channel_block(MOBA_O1, a_hi[:, KT:2 * KT], a_lo[:, KT:2 * KT])

            for n in range(2 * OUT0, 2 * OUT0 + 4):
                q = n - 2 * OUT0
                pe.wait_ge(lo_ready, n + 1)
                pe.wait_ge(merged_split, 2 if q < 2 else 4)
                if q < 2:
                    wait_bank_free(OUT0 + q)
                tiles = range(4) if q < 2 else range(4, 8)
                order = [(kk, t) for t in range(NT) for kk in range(4)] if q == 3 else None
                token_half([block_bank(OUT0 + q % 2, t) for t in range(NT)], n, tiles, q < 2, q >= 2, order,
                           out_chunk0 if q == 3 else None).then_inc(half_used, 1)
            for t in range(NT):
                for kh in range(2):
                    pe.wait_ge(xn2_ready, 2 * t + kh + 1)
                    transposes("h2", 2 * t + kh, [y_tok[:, t, P * k:P * k + P] for k in range(4 * kh, 4 * kh + 4)])

            def up_half(b, n, free, slot, jj, h):
                pe.wait_ge(lo_ready, n + 1)
                for t in range(NT):
                    wait_unit_read(pe, unit("h2", 2 * t + h))
                if h == 0:
                    pe.wait_ge(bank_read[jj], free)
                channel_half([bank[2 * jj], bank[2 * jj + 1]], slot, h_hi, h_lo, h).then_inc(half_used, 1)

            with pe.Fori(0, UP_BLOCKS // 2) as i:
                for jj in range(2):
                    for h in range(2):
                        up_half(UP0, i * 4 + (2 * UP0 + 2 * jj + h), i * 2 + UP0, 2 * jj + h, jj, h)
            for h in range(2):
                up_half(UP0 + UP_BLOCKS - 1, DOWN_FIRST_HALF - 2 + h, UP0 + UP_BLOCKS - 1, h, 0, h)

            for j in range(DOWN_HALVES):
                n = DOWN_FIRST_HALF + j
                pe.wait_ge(lo_ready, n + 1)
                pe.wait_ge(a_split, j + 1)
                hi = w_hi[n % SLOTS][:, :].rearrange("p (k n c) -> p k n c", k=2, n=2)
                lo = w_lo[n % SLOTS][:, :].rearrange("p (k n c) -> p k n c", k=2, n=2)
                last = j == DOWN_HALVES - 1
                if last:
                    pairs = [(kk, t, (c,)) for t in range(NT) for c in range(2) for kk in range(2)]
                else:
                    pairs = [(kk, t, (0, 1)) for kk in range(2) for t in range(NT)]
                for kk, t, cs in pairs:
                    k = 2 * j + kk
                    s_hi, s_lo = (a[:, k, P * t:P * t + P] for a in (a_hi, a_lo))
                    for c in cs:
                        mm(bank[4 + 2 * t + c][:, :], s_hi, hi[:, kk, c, :], start=(k == 0), stop=False)
                        mm(bank[4 + 2 * t + c][:, :], s_hi, lo[:, kk, c, :], start=False, stop=False)
                    for c in cs:
                        ins = mm(bank[4 + 2 * t + c][:, :], s_lo, hi[:, kk, c, :], start=False,
                                 stop=(k == D_FF // P - 1))
                    if last and kk == 1:
                        ins.then_inc(quarter_summed, 1)
                if not last:
                    ins.then_inc(half_used, 1)

        @block.scalar
        def _(act):
            A = nc.scalar.activation

            nc.scalar.preload_act_table(ACT.Square)
            act.dma_start(ident[:, :], ident_in).then_inc(ident_loaded, 16)
            act.dma_start(gain_row, gain_rows[0:1, :].partition_broadcast(P)).then_inc(gain_loaded, 16)

            def split(n, r=None, count=None):
                r = n % SLOTS if r is None else r
                act.wait_ge(raw_loaded[r], 16 * (n // SLOTS + 1) if count is None else count)
                if not isinstance(n, int) or n >= SLOTS:
                    act.wait_ge(half_used, n - (SLOTS - 1))
                A(w_hi[r][:, :], raw[r][:, :], ACT.Copy).then_inc(hi_ready, 1)

            def split_quarter(n, q):
                if n == 0 and q == 0:
                    act.wait_ge(raw_start, 16)
                elif q == (2 if n == 0 else 0):
                    act.wait_ge(raw_loaded[n], 16)
                c = slice(512 * q, 512 * q + 512)
                A(w_hi[n][:, c], raw[n][:, c], ACT.Copy).then_inc(piece_hi, 1)

            def h_read(j):
                kh, t = divmod(j, 2)
                act.wait_ge(unit_made, unit("h", j) + 1)
                A(h_hi[:, 4 * kh:4 * kh + 4, P * t:P * t + P],
                  ubank(unit("h", j))[:, :].rearrange("p (k s) -> p k s", k=4), ACT.Copy).then_inc(h_hi_ready, 1)

            act.wait_ge(x_loaded[0], 16)
            A(y_tok[:, 0, :], x_tok[:, 0, :], ACT.Square, accum_out=ss_x[:, 0:1]).then_inc(sums_x[0], 1)
            act.dma_start(rotary, rotary_in).then_inc(rotary_loaded, 16)
            split_quarter(0, 0)
            h_read(0)
            h_read(1)
            split_quarter(0, 1)
            split_quarter(0, 2)
            h_read(2)
            split_quarter(0, 3)
            h_read(3)
            for q in range(4):
                split_quarter(1, q)
            act.dma_start(decay, decay_in).then_inc(tables_loaded, 16)
            act.dma_start(mask[:, :], mask_in).then_inc(tables_loaded, 16)
            act.dma_start(col[:, :], cols).then_inc(tables_loaded, 16)
            for n in range(2, SLOTS):
                split(n)
            act.wait_ge(tables_loaded, 48)

            def copy_block(b, dst):
                for t in range(NT):
                    act.wait_ge(half_used, 2 * b + 2)
                    A(dst(t), block_bank(b, t)[:, :], ACT.Copy).then_inc(bank_read[b % 2], 1)

            def head_read(name, dst, gain):
                for t in range(NT):
                    u = unit(name, t)
                    act.wait_ge(unit_made, u + 1)
                    A(dst[:, :, P * t:P * t + P], ubank(u)[:, :].rearrange("p (h s) -> p h s", h=4),
                      ACT.Identity, scale=col[:, gain:gain + 1]).then_inc(unit_read[u % 4], 1)

            def silu_gates(b):
                act.wait_ge(half_used, 2 * b + 2)
                for j in range(2):
                    k = 4 * (b - G_R0) + 2 * j
                    A(g_t[:, k:k + 2, :], block_bank(b, j)[:, :].rearrange("p (m s) -> p m s", m=2), ACT.Silu)\
                        .then_inc(bank_read[b % 2], 1)

            def square_heads(b):
                act.wait_ge(half_used, 2 * b + 2)
                if b > Q_M0:
                    act.wait_ge(sums_qk, 2 * (b - Q_M0))
                for t in range(NT):
                    for h in range(4):
                        ins = A(discard[:, 4 * t + h, :], block_bank(b, t)[:, HEAD * h:HEAD * h + HEAD], ACT.Square,
                                accum_out=ss_qk[:, b - Q_M0, 4 * t + h:4 * t + h + 1])
                    ins.then_inc(sums_qk, 1)

            def sigmoid_gates(b, first, bias):
                act.wait_ge(half_used, 2 * b + 2)
                for j in range(2):
                    if first == GATE_M0:
                        wait_bank_read(act, RET_O1, 1)
                    for i in range(2):
                        k = 4 * (b - first) + 2 * j + i
                        c = COL_GATE_BIAS + bias + k
                        ins = A(gates[:, k, :], block_bank(b, j)[:, SEQ * i:SEQ * i + SEQ], ACT.Sigmoid,
                                bias=col[:, c:c + 1])
                    ins.then_inc(bank_read[b % 2], 1)

            def ret_read(g):
                for j in range(2):
                    u = unit(f"ret_t{g}", j)
                    act.wait_ge(unit_made, u + 1)
                    for i in range(2):
                        k = 4 * g + 2 * j + i
                        ins = A(ret_t[:, k, :], ubank(u)[:, SEQ * i:SEQ * i + SEQ], ACT.Identity,
                                scale=col[:, COL_RET_GAIN + k:COL_RET_GAIN + k + 1],
                                bias=col[:, COL_RET_BIAS + k:COL_RET_BIAS + k + 1])
                    ins.then_inc(unit_read[u % 4], 1)
                for j in range(2 * g, 2 * g + 2):
                    act.wait_ge(ret_gated, j + 1)
                    A(a_hi[:, 2 * j:2 * j + 2, :], ret_t[:, 2 * j:2 * j + 2, :], ACT.Copy).then_inc(ret_hi_ready, 1)

            def exps(g):
                act.wait_ge(neg_max_ready, g + 1)
                for j in range(4):
                    for c, (lo_c, hi_c) in enumerate(((0, P), (P, P + SEQ))):
                        i = 8 * g + 2 * j + c
                        ins = A(probs[g][:, j, lo_c:hi_c], probs[g][:, j, lo_c:hi_c], ACT.Exp, scale=QK_SCALE,
                                bias=neg_max[:, i:i + 1], accum_out=row_sum[:, i:i + 1])
                ins.then_inc(exp_done, 1)

            def probs_read(g):
                for j in range(4):
                    u = unit(f"probs{g}", j)
                    act.wait_ge(unit_made, u + 1)
                    A(probs_t[:, 4 * g + j, :], ubank(u)[:, 0:3 * P], ACT.Copy).then_inc(unit_read[u % 4], 1)

            def attn_read(g):
                for j in range(2):
                    u = unit(f"moba_out{g}", j)
                    k = KT + 4 * g + 2 * j
                    act.wait_ge(unit_made, u + 1)
                    A(a_hi[:, k:k + 2, :], ubank(u)[:, :].rearrange("p (m s) -> p m s", m=2), ACT.Copy)\
                        .then_inc(attn_hi_ready, 1)

            def merged_high(b):
                for j in range(2):
                    i = 2 * (b - MOBA_O0) + j
                    act.wait_ge(merged_ready, i + 1)
                    A(h_hi[:, 2 * i:2 * i + 2, :], merged[:, 2 * i:2 * i + 2, :], ACT.Copy).then_inc(merged_hi_ready, 1)

            def square_x2(b):
                for t in range(NT):
                    c = 512 * (b - OUT0)
                    wait_bank_read(act, b, t)
                    A(y_tok[:, t, c:c + 512], x_tok[:, t, c:c + 512], ACT.Square,
                      accum_out=ss_x2[:, 2 * (b - OUT0) + t:2 * (b - OUT0) + t + 1]).then_inc(sums_x2, 1)

            def h2_high():
                for j in (0, 2, 1, 3):
                    t, kh = divmod(j, 2)
                    u = unit("h2", j)
                    act.wait_ge(unit_made, u + 1)
                    A(h_hi[:, 4 * kh:4 * kh + 4, P * t:P * t + P],
                      ubank(u)[:, :].rearrange("p (k s) -> p k s", k=4), ACT.Copy).then_inc(h2_hi_ready[kh], 1)

            first = {
                V_R0: lambda: copy_block(V_R0, lambda t: v_r[:, t, 0:512]),
                V_R1: lambda: copy_block(V_R1, lambda t: v_r[:, t, 512:1024]),
                G_R0: lambda: silu_gates(G_R0), G_R1: lambda: silu_gates(G_R1),
                Q_M0: lambda: square_heads(Q_M0),
                Q_M1: lambda: (head_read("q_m0", qm_t[:, 0:4], COL_Q_GAIN), square_heads(Q_M1)),
                K_M0: lambda: (head_read("q_m1", qm_t[:, 4:8], COL_Q_GAIN), square_heads(K_M0)),
                K_M1: lambda: (head_read("k_m0", km_t[:, 0:4], COL_K_GAIN), square_heads(K_M1)),
                V_M0: lambda: (head_read("k_m1", km_t[:, 4:8], COL_K_GAIN),
                               copy_block(V_M0, lambda t: v_m[:, t, 0:512])),
                V_M1: lambda: copy_block(V_M1, lambda t: v_m[:, t, 512:1024]),
                GATE_R0: lambda: exps(1),
                GATE_R1: lambda: sigmoid_gates(GATE_R1, GATE_R0, 0),
                RET_O0: lambda: (attn_read(0), probs_read(1)), RET_O1: lambda: attn_read(1),
                GATE_M0: lambda: sigmoid_gates(GATE_M0, GATE_M0, KT),
                GATE_M1: lambda: sigmoid_gates(GATE_M1, GATE_M0, KT),
                MOBA_O0: lambda: merged_high(MOBA_O0), MOBA_O1: lambda: merged_high(MOBA_O1),
                OUT0: lambda: square_x2(OUT0), OUT1: lambda: (square_x2(OUT1), h2_high()),
            }
            second = {
                Q_M1: lambda: ret_read(0), K_M0: lambda: ret_read(1),
                V_M1: lambda: exps(0),
                GATE_R0: lambda: sigmoid_gates(GATE_R0, GATE_R0, 0),
                GATE_R1: lambda: probs_read(0),
            }
            for b in range(UP0):
                if b == OUT0:
                    split(2 * b + 4)
                    split(2 * b + 5)
                first.get(b, lambda: None)()
                if b != OUT0:
                    split(2 * b + 4)
                    second.get(b, lambda: None)()
                    split(2 * b + 5)

            def up_read(jj, used, conv_before, read, conv_col):
                act.wait_ge(half_used, used)
                act.wait_ge(prod_ready, conv_before)
                for j in range(2):
                    A(u_in[:, jj, 2 * j:2 * j + 2, PAD:PAD + SEQ],
                      bank[2 * jj + j][:, :].rearrange("p (m s) -> p m s", m=2), ACT.Copy)
                    for i in range(2):
                        m = 2 * j + i
                        ins = A(conv[:, jj, m, :], bank[2 * jj + j][:, SEQ * i:SEQ * i + SEQ], ACT.Identity,
                                scale=conv_col(4 * m + 2), bias=conv_col(4 * m + 3))
                    ins.then_inc(bank_read[jj], 1)
                act.wait_ge(conv_gate_done, read)
                A(conv[:, jj, 0:2, :], conv[:, jj, 0:2, :], ACT.Silu).then_inc(silu_done, 1)

            def up_high(jj, k, ready):
                act.wait_ge(prod_ready, ready)
                A(a_hi[:, k, :], prod[:, jj, :, :], ACT.Copy).then_inc(a_hi_ready, 1)

            nc.scalar.preload_act_table(ACT.Silu)
            with act.Fori(0, UP_BLOCKS // 2) as i:
                for jj in range(2):
                    up_read(jj, i * 4 + (2 * UP0 + 2 * jj + 2), i * 2 + (jj + 1),
                            i * 2 + (jj + 1), lambda c: col[:, bass.ds(i * 32 + (COL_CONV + 16 * jj + c), 1)])
                    r = 2 * jj
                    split(i * 4 + (2 * UP0 + 4 + r), r, i * 16 + 16 * ((2 * UP0 + 4) // SLOTS + 1))
                    up_high(jj, bass.ds(i * 4 + 2 * jj, 2), i * 2 + (jj + 3))
                    r = 2 * jj + 1
                    split(i * 4 + (2 * UP0 + 4 + r), r, i * 16 + 16 * ((2 * UP0 + 4) // SLOTS + 1))
            b = UP_BLOCKS - 1
            up_read(0, DOWN_FIRST_HALF, b + 1, b + 1,
                    lambda c: col[:, COL_CONV + 16 * b + c:COL_CONV + 16 * b + c + 1])
            up_high(0, slice(2 * b, 2 * b + 2), b + 3)
            for n in range(DOWN_FIRST_HALF + 2, HALVES):
                split(n)

        @block.vector
        def _(dve):
            tt = nc.vector.tensor_tensor
            ts = nc.vector.tensor_scalar
            stt = nc.vector.scalar_tensor_tensor
            done = [0]

            def step(ins):
                done[0] += 1
                ins.then_inc(dve_step, 1)
                dve.wait_ge(dve_step, done[0])

            def split(n, r=None):
                r = n % SLOTS if r is None else r
                dve.wait_ge(hi_ready, n - 1)
                tt(w_lo[r][:, :], raw[r][:, :], w_hi[r][:, :].bitcast(f32), ALU.subtract).then_inc(lo_ready, 1)

            def split_quarter(n, q):
                dve.wait_ge(piece_hi, 4 * n + q + 1)
                c = slice(512 * q, 512 * q + 512)
                tt(w_lo[n][:, c], raw[n][:, c], w_hi[n][:, c].bitcast(f32), ALU.subtract)\
                    .then_inc(piece_lo if q < 3 else lo_ready, 1)

            def normalise(c, t):
                if c == 0:
                    dve.wait_ge(inv_x_ready, t + 1)
                stt(out=y_tok[:, t, 512 * c:512 * c + 512], in0=x_tok[:, t, 512 * c:512 * c + 512],
                    scalar=inv_x[:, t:t + 1], in1=gain_row[:, 512 * c:512 * c + 512],
                    op0=ALU.mult, op1=ALU.mult).then_inc(xn_ready, 1)

            def h_rest(j):
                kh, t = divmod(j, 2)
                u = unit("h", j)
                dve.wait_ge(h_hi_ready, j + 1)
                part = (slice(None), slice(4 * kh, 4 * kh + 4), slice(P * t, P * t + P))
                tt(h_lo[part], ubank(u)[:, :].rearrange("p (k s) -> p k s", k=4), h_hi[part].bitcast(f32),
                   ALU.subtract).then_inc(unit_read[u % 4], 1)

            nc.vector.memset(w_lo[SLOTS - 1][:, 0:512].bitcast(f32), 0.0).then_inc(zeros_ready, 1)
            dve.wait_ge(x_loaded[1], 16)
            nc.vector.tensor_tensor_reduce(out=y_tok[:, 1, :], in0=x_tok[:, 1, :], in1=x_tok[:, 1, :], scale=1.0,
                                           scalar=0.0, op0=ALU.mult, op1=ALU.add,
                                           accum_out=ss_x[:, 1:2]).then_inc(sums_x[1], 1)
            dve.wait_ge(gain_loaded, 16)
            for job, *args in ((normalise, 0, 0), (normalise, 0, 1), (split_quarter, 0, 0),
                               (h_rest, 0), (h_rest, 1), (normalise, 1, 0), (split_quarter, 0, 1), (normalise, 1, 1),
                               (split_quarter, 0, 2), (h_rest, 2), (split_quarter, 0, 3), (h_rest, 3),
                               (split_quarter, 1, 0), (split_quarter, 1, 1), (split_quarter, 1, 2),
                               (split_quarter, 1, 3)):
                job(*args)
            for n in range(2, SLOTS):
                split(n)
            dve.wait_ge(rotary_loaded, 16)
            dve.wait_ge(tables_loaded, 48)

            def rotate(b):
                dve.wait_ge(half_used, 2 * b + 2)
                half = RET_QK // 2
                tmp = xs[:, 0:512].rearrange("p (h s) -> p h s", h=2)

                def spread(table, a, z):
                    return table[a:z, :].unsqueeze(1).broadcast_to([z - a, 2, SEQ])

                for j in range(2):
                    ps = block_bank(b, j)[:, :].rearrange("p (h s) -> p h s", h=2)
                    dst = (qr_t if b == Q_R else kr_t)[:, 2 * j:2 * j + 2, :]
                    tt(dst, ps, spread(cos_t, 0, P), ALU.mult)
                    tt(tmp[0:half], ps[half:P], spread(sin_t, half, P), ALU.mult)
                    tt(tmp[half:P], ps[0:half], spread(sin_t, 0, half), ALU.mult).then_inc(bank_read[b % 2], 1)
                    wait_bank_read(dve, b, j)
                    tt(dst, dst, tmp, ALU.add).then_inc(rot_ready, 1)
                    dve.wait_ge(rot_ready, 2 * (b - Q_R) + j + 1)

            def decays():
                for h in range(RET_HEADS):
                    u = unit("ret_scores", h)
                    dve.wait_ge(unit_made, u + 1)
                    tt(ret_probs[:, h, :], ubank(u)[:, 0:3 * P], decay[:, 3 * P * h:3 * P * h + 3 * P], ALU.mult)\
                        .then_inc(unit_read[u % 4], 1)

            def group_stats():
                for h in range(RET_HEADS):
                    dve.wait_ge(unit_made, unit("ret_out", h) + 1)
                    for t in range(NT):
                        ins = nc.vector.bn_stats(gn_stats[:, 2 * h + t, :],
                                                 ubank(unit("ret_out", h))[:, RET_V * t:RET_V * t + RET_V])
                step(ins)
                for i in range(8):
                    ins = nc.vector.bn_aggr(gn_mv[:, i, :], gn_stats[:, i, :])
                ins.then_inc(gn_stats_ready, 1)
                dve.wait_ge(gn_stats_ready, 1)

            def group_norm():
                dve.wait_ge(gn_rstd_ready, 1)
                for h in range(RET_HEADS):
                    u = unit("ret_out", h)
                    for t in range(NT):
                        i = 2 * h + t
                        ins = ts(y_tok[:, t, RET_V * h:RET_V * h + RET_V], ubank(u)[:, RET_V * t:RET_V * t + RET_V],
                                 gn_mv[:, i, 0:1], gn_rstd[:, i:i + 1], ALU.subtract, ALU.mult)
                    ins.then_inc(unit_read[u % 4], 1)

            def qk_norm(b):
                q = b - Q_M0
                dve.wait_ge(inv_qk_ready, q + 1)
                if q >= 2:
                    dve.wait_ge(unit_made, unit(f"q_m{q - 2}", 1) + 1)
                for t in range(NT):
                    tt(qn[:, q % 2, t].rearrange("p (h d) -> p h d", h=4),
                       block_bank(b, t)[:, :].rearrange("p (h d) -> p h d", h=4),
                       inv_qk[:, q, 4 * t:4 * t + 4].unsqueeze(2).broadcast_to([P, 4, HEAD]), ALU.mult)\
                        .then_inc(bank_read[b % 2], 1)

            def ret_gate(g):
                for j in range(2 * g, 2 * g + 2):
                    wait_unit_read(dve, unit(f"ret_t{g}", j % 2))
                    k = slice(2 * j, 2 * j + 2)
                    tt(ret_t[:, k, :], ret_t[:, k, :], g_t[:, k, :], ALU.mult).then_inc(ret_gated, 1)

            def ret_low(g):
                for j in range(2 * g, 2 * g + 2):
                    k = slice(2 * j, 2 * j + 2)
                    dve.wait_ge(ret_hi_ready, j + 1)
                    tt(a_lo[:, k, :], ret_t[:, k, :], a_hi[:, k, :].bitcast(f32), ALU.subtract).then_inc(ret_split, 1)

            def masked_max(g):
                for j in range(4):
                    u = unit(f"scores{g}", j)
                    dve.wait_ge(unit_made, u + 1)
                    for c, (lo_c, hi_c) in enumerate(((0, P), (P, P + SEQ))):
                        i = 8 * g + 2 * j + c
                        ins = nc.vector.tensor_tensor_reduce(
                            out=probs[g][:, j, lo_c:hi_c], in0=ubank(u)[:, lo_c:hi_c],
                            in1=mask[:, 2 * P - (hi_c - lo_c):2 * P], scale=1.0, scalar=MASKED,
                            op0=ALU.add, op1=ALU.max, accum_out=row_max[:, i:i + 1])
                    ins.then_inc(unit_read[u % 4], 1)
                wait_unit_read(dve, unit(f"scores{g}", 3))
                ts(neg_max[:, 8 * g:8 * g + 8], row_max[:, 8 * g:8 * g + 8], -QK_SCALE, None, ALU.mult)\
                    .then_inc(neg_max_ready, 1)

            def normalise_probs(g):
                dve.wait_ge(exp_done, g + 1)
                step(nc.vector.reciprocal(inv_sum[:, 8 * g:8 * g + 8], row_sum[:, 8 * g:8 * g + 8]))
                for j in range(4):
                    for c, (lo_c, hi_c) in enumerate(((0, P), (P, P + SEQ))):
                        i = 8 * g + 2 * j + c
                        ins = ts(probs[g][:, j, lo_c:hi_c], probs[g][:, j, lo_c:hi_c], inv_sum[:, i:i + 1], None,
                                 ALU.mult)
                    ins.then_inc(probs_ready, 1)

            def attn_low(g):
                for j in range(2):
                    u = unit(f"moba_out{g}", j)
                    k = slice(KT + 4 * g + 2 * j, KT + 4 * g + 2 * j + 2)
                    dve.wait_ge(attn_hi_ready, 2 * g + j + 1)
                    tt(a_lo[:, k, :], ubank(u)[:, :].rearrange("p (m s) -> p m s", m=2), a_hi[:, k, :].bitcast(f32),
                       ALU.subtract).then_inc(unit_read[u % 4], 1)

            def gate_ret(b):
                dve.wait_ge(half_used, 2 * b + 2)
                if b == RET_O0:
                    dve.wait_ge(unit_made, unit("probs1", 3) + 1)
                    wait_bank_read(dve, GATE_R0, 1)
                    wait_bank_read(dve, GATE_R1, 1)
                for j in range(2):
                    k = slice(4 * (b - RET_O0) + 2 * j, 4 * (b - RET_O0) + 2 * j + 2)
                    tt(merged[:, k, :], block_bank(b, j)[:, :].rearrange("p (m s) -> p m s", m=2), gates[:, k, :],
                       ALU.mult).then_inc(bank_read[b % 2], 1)
                wait_bank_read(dve, b, 1)

            def gate_moba(b):
                dve.wait_ge(half_used, 2 * b + 2)
                if b == MOBA_O0:
                    wait_bank_read(dve, GATE_M0, 1)
                    wait_bank_read(dve, GATE_M1, 1)
                for j in range(2):
                    i = 2 * (b - MOBA_O0) + j
                    k = slice(2 * i, 2 * i + 2)
                    tt(gates[:, k, :], block_bank(b, j)[:, :].rearrange("p (m s) -> p m s", m=2), gates[:, k, :],
                       ALU.mult).then_inc(bank_read[b % 2], 1)
                    wait_bank_read(dve, b, j)
                    tt(merged[:, k, :], merged[:, k, :], gates[:, k, :], ALU.add).then_inc(merged_ready, 1)
                for j in range(2):
                    i = 2 * (b - MOBA_O0) + j
                    k = slice(2 * i, 2 * i + 2)
                    dve.wait_ge(merged_hi_ready, i + 1)
                    tt(h_lo[:, k, :], merged[:, k, :], h_hi[:, k, :].bitcast(f32), ALU.subtract)\
                        .then_inc(merged_split, 1)

            def residual(b):
                for t in range(NT):
                    if b == OUT0:
                        dve.wait_ge(half_used, 2 * OUT0 + 3)
                        dve.wait_ge(x_again, 16)
                    elif t == 0:
                        dve.wait_ge(out_chunk0, 1)
                    else:
                        dve.wait_ge(half_used, 2 * OUT0 + 4)
                    c = 512 * (b - OUT0)
                    tt(x_tok[:, t, c:c + 512], block_bank(b, t)[:, :], x_tok[:, t, c:c + 512], ALU.add)\
                        .then_inc(bank_read[b % 2], 1)

            def norm2():
                dve.wait_ge(gain2_loaded, 16)
                for t in range(NT):
                    dve.wait_ge(inv_x2_ready, t + 1)
                    for c in range(2):
                        stt(out=y_tok[:, t, 512 * c:512 * c + 512], in0=x_tok[:, t, 512 * c:512 * c + 512],
                            scalar=inv_x2[:, t:t + 1], in1=gain_row[:, 512 * c:512 * c + 512],
                            op0=ALU.mult, op1=ALU.mult).then_inc(xn2_ready, 1)
                for j in (0, 2, 1, 3):
                    t, kh = divmod(j, 2)
                    u = unit("h2", j)
                    dve.wait_ge(h2_hi_ready[kh], t + 1)
                    part = (slice(None), slice(4 * kh, 4 * kh + 4), slice(P * t, P * t + P))
                    tt(h_lo[part], ubank(u)[:, :].rearrange("p (k s) -> p k s", k=4), h_hi[part].bitcast(f32),
                       ALU.subtract).then_inc(unit_read[u % 4], 1)
                for jj in range(2):
                    nc.vector.memset(u_in[:, jj, :, 0:PAD], 0.0).then_inc(prod_ready, 1)
                dve.wait_ge(prod_ready, 2)

            first = {
                Q_R: lambda: rotate(Q_R), K_R: lambda: rotate(K_R),
                G_R0: decays, G_R1: group_stats,
                V_M1: lambda: masked_max(0), GATE_R0: lambda: masked_max(1),
                RET_O0: lambda: attn_low(0), RET_O1: lambda: (gate_ret(RET_O1), attn_low(1)),
                MOBA_O0: lambda: gate_moba(MOBA_O0), MOBA_O1: lambda: gate_moba(MOBA_O1),
                OUT0: lambda: residual(OUT0), OUT1: lambda: (residual(OUT1), norm2()),
            }
            second = {
                G_R1: group_norm,
                Q_M0: lambda: qk_norm(Q_M0), Q_M1: lambda: (qk_norm(Q_M1), ret_gate(0), ret_low(0)),
                K_M0: lambda: (qk_norm(K_M0), ret_gate(1), ret_low(1)),
                K_M1: lambda: qk_norm(K_M1),
                V_M1: lambda: normalise_probs(0), GATE_R0: lambda: normalise_probs(1),
                RET_O0: lambda: gate_ret(RET_O0),
            }
            for b in range(UP0):
                if b == OUT0:
                    split(2 * b + 4)
                    split(2 * b + 5)
                first.get(b, lambda: None)()
                if b != OUT0:
                    split(2 * b + 4)
                    second.get(b, lambda: None)()
                    split(2 * b + 5)

            def up_conv(jj, read, silu, conv_col, conv_steps):
                for j in range(2):
                    dve.wait_ge(bank_read[jj], read(j))
                    for tap in (1, 0):
                        for i in range(2):
                            m = 2 * j + i
                            ins = stt(out=conv[:, jj, m, :], in0=u_in[:, jj, m, tap:tap + SEQ],
                                      scalar=conv_col(4 * m + tap), in1=conv[:, jj, m, :], op0=ALU.mult, op1=ALU.add)
                        if tap or j:
                            ins.then_inc(dve_step, 1)
                            dve.wait_ge(dve_step, conv_steps(2 * j + 1 - tap if j else 0))
                        else:
                            ins.then_inc(conv_gate_done, 1)
                dve.wait_ge(silu_done, silu)
                tt(prod[:, jj, :, :], conv[:, jj, 0:2, :], conv[:, jj, 2:4, :], ALU.mult).then_inc(prod_ready, 1)

            def up_low(jj, k, ready):
                dve.wait_ge(a_hi_ready, ready)
                tt(a_lo[:, k, :], prod[:, jj, :, :], a_hi[:, k, :].bitcast(f32), ALU.subtract).then_inc(a_split, 1)

            steps0 = done[0]
            order = {0: 1, 2: 2, 3: 3}
            with dve.Fori(0, UP_BLOCKS // 2) as i:
                for jj in range(2):
                    up_conv(jj, lambda j: i * 2 + (UP0 + j + 1), i * 2 + (jj + 1),
                            lambda c: col[:, bass.ds(i * 32 + (COL_CONV + 16 * jj + c), 1)],
                            lambda s: i * 6 + (steps0 + 3 * jj + order[s]))
                    r = 2 * jj
                    split(i * 4 + (2 * UP0 + 4 + r), r)
                    up_low(jj, bass.ds(i * 4 + 2 * jj, 2), i * 2 + (jj + 1))
                    r = 2 * jj + 1
                    split(i * 4 + (2 * UP0 + 4 + r), r)
            b = UP_BLOCKS - 1
            up_conv(0, lambda j: UP0 + b + j + 1, b + 1,
                    lambda c: col[:, COL_CONV + 16 * b + c:COL_CONV + 16 * b + c + 1],
                    lambda s: steps0 + 3 * b + order[s])
            up_low(0, slice(2 * b, 2 * b + 2), b + 1)
            for n in range(DOWN_FIRST_HALF + 2, HALVES):
                split(n)
            for t in range(NT):
                for c in range(2):
                    dve.wait_ge(quarter_summed, 2 * t + c + 1)
                    tt(y_tok[:, t, 512 * c:512 * c + 512], bank[4 + 2 * t + c][:, :],
                       x_tok[:, t, 512 * c:512 * c + 512], ALU.add).then_inc(out_ready, 1)


def _block_halves(w, columns):
    m = w[:, columns].reshape(2, 4, P, BLOCK_COLS).transpose(0, 2, 1, 3)
    return [m[0].reshape(P, HALF_ELEMS), m[1].reshape(P, HALF_ELEMS)]


def _columns(v):
    return v.reshape(-1, P).T


def _pack_weights(w_in, w_gate, w_ret_o, w_moba_o, w_out, w_up, w_down):
    halves = []
    cut = [slice(BLOCK_COLS * i, BLOCK_COLS * (i + 1)) for i in range(12)]
    for i in (2, 3, 0, 1, *range(4, 12)):
        halves += _block_halves(w_in, cut[i])
    for w, i in ((w_gate, 0), (w_gate, 1), (w_ret_o, 0), (w_ret_o, 1), (w_gate, 2), (w_gate, 3),
                 (w_moba_o, 0), (w_moba_o, 1)):
        halves += _block_halves(w, cut[i])
    o0, o1 = (_block_halves(w_out, cut[i]) for i in range(2))
    halves += [o0[0], o1[0], o0[1], o1[1]]
    for j in range(UP_BLOCKS):
        c = np.r_[UP_COLS * j:UP_COLS * (j + 1), D_FF + UP_COLS * j:D_FF + UP_COLS * (j + 1)]
        halves += _block_halves(w_up, c)
    down = w_down.reshape(DOWN_HALVES, 2, P, D).transpose(0, 2, 1, 3).reshape(DOWN_HALVES, P, HALF_ELEMS)
    return np.ascontiguousarray(np.concatenate([np.stack(halves), down]))


def _tables():
    half = RET_QK // 2
    inv_freq = np.power(np.float32(10000.0), -np.arange(half, dtype=np.float32) / np.float32(half))
    ang = (np.arange(SEQ, dtype=np.float32)[:, None] * inv_freq[None, :].astype(np.float32)).astype(np.float64)
    cos, sin = np.cos(ang).T, np.sin(ang).T
    rotary = np.concatenate([np.concatenate([cos, cos]), np.concatenate([sin, -sin])], 1).astype(np.float32)
    key, query = np.arange(P)[:, None], np.arange(SEQ)[None, :]
    decay = np.zeros((P, RET_HEADS, 3 * P))
    for h in range(RET_HEADS):
        d = np.where(query >= key, np.exp(np.log1p(-2.0 ** (-5.0 - h)) * np.maximum(query - key, 0)), 0.0)
        decay[:, h, 0:SEQ] = d
        decay[:, h, SEQ:] = d[:, 0:P]
    decay = (decay * RET_QK ** -0.5).reshape(P, -1).astype(np.float32)
    mask = np.zeros((P, 2 * P), np.float32)
    mask[:, P:] = np.where(np.arange(P)[None, :] <= np.arange(P)[:, None], 0.0, MASKED)
    return rotary, decay, mask, np.eye(P, dtype=np.float32)


def kernel(x, attn_norm, w_in, ret_norm_gain, ret_norm_bias, moba_q_gain, moba_k_gain, w_ret_o, w_moba_o,
           w_gate, b_gate, w_out, ffn_norm, w_up, conv_w, conv_b, w_down):
    import concourse.bacc as bacc
    from concourse.bass_utils import run_bass_kernel_spmd

    a = {k: np.asarray(v) for k, v in locals().items() if k not in ("bacc", "run_bass_kernel_spmd")}
    taps = np.concatenate([a["conv_w"][0], a["conv_b"][0][None]]).reshape(4, 2, UP_BLOCKS, 2, P)
    conv_cols = taps.transpose(4, 2, 1, 3, 0).reshape(P, CONV_COLS)
    rotary, decay, mask, eye = _tables()
    arrays = {
        "x": a["x"][0],
        "weights": _pack_weights(*(a[n][0] for n in ("w_in", "w_gate", "w_ret_o", "w_moba_o", "w_out", "w_up",
                                                     "w_down"))),
        "gain_rows": np.stack([a["attn_norm"][0], a["ffn_norm"][0]]),
        "cols": np.concatenate([_columns(a["moba_q_gain"][0]), _columns(a["moba_k_gain"][0]),
                                _columns(a["ret_norm_gain"][0]), _columns(a["ret_norm_bias"][0]),
                                _columns(a["b_gate"][0]), conv_cols], 1),
        "ident": eye, "mask": mask, "rotary": rotary, "decay": decay,
    }
    nc = bacc.Bacc("TRN2", target_bir_lowering=False, num_devices=1)
    arrays = {f"{k}_dram": np.ascontiguousarray(v) for k, v in arrays.items()}
    args = [nc.dram_tensor(k, v.shape, mybir.dt.from_np(v.dtype), kind="ExternalInput").ap()
            for k, v in arrays.items()]
    out = nc.dram_tensor("out_dram", (SEQ, D), mybir.dt.float32, kind="ExternalOutput").ap()
    hybrid_layer(nc, *args, out)
    r = run_bass_kernel_spmd(nc, [arrays], core_ids=[0])
    return r.results[0]["out_dram"].reshape(1, SEQ, D)
```
